# Optimizing a Trainium2 kernel written in Bass

```python
import jax, jax.numpy as jnp
from jax import lax
import numpy as np

D_MODEL = 1024
BATCH = 1
SEQ = 256
DEPTH = 2
DEC_BATCH = 8
DEC_SEQ = 4
PAST_LEN = 1024
PAGE_SIZE = 128

N_A_LAYERS = DEPTH // 2
N_B_LAYERS = DEPTH - N_A_LAYERS
EPS = 1e-6
NEG = -1e30

CHUNK = 128
D_AV = 2 * D_MODEL
A_GROUPS = 8
A_GROUP_DIM = D_AV // A_GROUPS

HEAD_DIM = 64
WINDOWS = (128, 512, 2048)
DILATIONS = (1, 4, 16)
N_GROUPS_B = len(WINDOWS)
HPG = 4
N_HEADS_B = N_GROUPS_B * HPG
ATT_W = N_HEADS_B * HEAD_DIM

PEER_HEADS = 8
N_KEYS = 128
N_EXPERTS = N_KEYS * N_KEYS
D_QUERY = 256
D_HALF = D_QUERY // 2
PEER_TOPK = 16
PEER_BLOCK = 256

kernel_name = "yoco_gmlp_dilated_peer_step"

def rmsnorm(x, g):
    xf = x.astype(jnp.float32)
    y = xf * lax.rsqrt(jnp.mean(xf * xf, axis=-1, keepdims=True) + EPS)
    return (y * g.astype(jnp.float32)).astype(x.dtype)

def alibi_slopes():
    return jnp.asarray(2.0 ** (-8.0 * np.arange(1, N_HEADS_B + 1) / N_HEADS_B), dtype=jnp.float32)

def chunk_spatial_mix(v, w_s, b_s):
    B, L = v.shape[:2]
    n_chunks = -(-L // CHUNK)
    c = CHUNK if n_chunks > 1 else L
    lp = n_chunks * c
    vp = jnp.pad(v, ((0, 0), (0, lp - L), (0, 0), (0, 0))).reshape(B, n_chunks, c, A_GROUPS, A_GROUP_DIM)
    causal = jnp.tril(jnp.ones((c, c), dtype=bool))
    w = jnp.where(causal[None], w_s[:, :c, :c], 0)
    mixed = jnp.einsum('gts,bnsgc->bntgc', w, vp) + b_s[:, :c].T[None, None, :, :, None]
    return mixed.reshape(B, lp, A_GROUPS, A_GROUP_DIM)[:, :L]

def mixer_a(h, w_in, v_norm, w_s, b_s, w_out):
    z = jax.nn.gelu(h @ w_in)
    u, v = jnp.split(z, 2, axis=-1)
    v = rmsnorm(v, v_norm)
    B, L = v.shape[:2]
    gate = chunk_spatial_mix(v.reshape(B, L, A_GROUPS, A_GROUP_DIM), w_s, b_s).reshape(B, L, D_AV)
    out = (u * gate) @ w_out
    rows = L - ((L - 1) // CHUNK) * CHUNK
    return out, v[:, L - rows:]

def peer_block(h, w_q, sub_keys, u_tab, v_tab):
    T = h.shape[0]
    q = (h @ w_q).reshape(T, PEER_HEADS, 2, D_HALF)
    s = jnp.einsum('thpe,pke->thpk', q, sub_keys).astype(jnp.float32)
    s1, i1 = lax.top_k(s[:, :, 0], PEER_TOPK)
    s2, i2 = lax.top_k(s[:, :, 1], PEER_TOPK)
    cand = (s1[..., :, None] + s2[..., None, :]).reshape(T, PEER_HEADS, PEER_TOPK * PEER_TOPK)
    top_s, top_c = lax.top_k(cand, PEER_TOPK)
    e1 = jnp.take_along_axis(i1, top_c // PEER_TOPK, axis=-1)
    e2 = jnp.take_along_axis(i2, top_c % PEER_TOPK, axis=-1)
    expert = e1 * N_KEYS + e2
    g = jax.nn.softmax(top_s, axis=-1)
    a = jnp.einsum('td,thkd->thk', h, u_tab[expert]).astype(jnp.float32)
    coef = (g * jax.nn.gelu(a)).astype(h.dtype)
    return jnp.einsum('thk,thkd->td', coef, v_tab[expert])

def peer(x, w_q, sub_keys, u_tab, v_tab):
    B, L, D = x.shape
    T = B * L
    n_blk = -(-T // PEER_BLOCK)
    xt = jnp.pad(x.reshape(T, D), ((0, n_blk * PEER_BLOCK - T), (0, 0))).reshape(n_blk, PEER_BLOCK, D)
    y = lax.map(lambda hb: peer_block(hb, w_q, sub_keys, u_tab, v_tab), xt)
    return y.reshape(n_blk * PEER_BLOCK, D)[:T].reshape(B, L, D)

def dilated_attn_prompt(q, k, v, window, dil, slopes):
    B, T, HG, HD = q.shape
    span = window // dil
    blk = span
    unit = dil * blk
    tp = -(-T // unit) * unit
    nb = tp // unit

    def split(a):
        a = jnp.pad(a, ((0, 0), (0, tp - T), (0, 0), (0, 0)))
        return a.reshape(B, nb, blk, dil, HG, HD)

    def with_prev(a):
        prev = jnp.pad(a, ((0, 0), (1, 0), (0, 0), (0, 0), (0, 0), (0, 0)))[:, :-1]
        return jnp.concatenate([prev, a], axis=2)

    qb = split(q)
    kk, vv = with_prev(split(k)), with_prev(split(v))
    s = jnp.einsum('bnqrhe,bnkrhe->bnrhqk', qb, kk).astype(jnp.float32) * HD ** -0.5
    tap = blk + jnp.arange(blk)[:, None] - jnp.arange(2 * blk)[None, :]
    in_win = (tap >= 0) & (tap <= span)
    exists = (jnp.arange(nb)[:, None] > 0) | (jnp.arange(2 * blk)[None, :] >= blk)
    mask = in_win[None] & exists[:, None, :]
    bias = -slopes[:, None, None] * (tap * dil).astype(jnp.float32)[None]
    s = jnp.where(mask[None, :, None, None], s + bias[None, None, None], NEG)
    lse = jax.nn.logsumexp(s, axis=-1)
    p = jnp.exp(s - lse[..., None])
    o = jnp.einsum('bnrhqk,bnkrhe->bnqrhe', p.astype(vv.dtype), vv)
    o = o.reshape(B, tp, HG, HD)[:, :T]
    lse = lse.transpose(0, 1, 4, 2, 3).reshape(B, tp, HG)[:, :T]
    return o, lse

def dilated_attn_sample(q, k_new, v_new, cache, window, dil, slopes):
    S, HD = q.shape[1], q.shape[3]
    L = cache.shape[1]
    span = window // dil
    keys = jnp.concatenate([cache[:, :, 0], k_new], axis=1)
    vals = jnp.concatenate([cache[:, :, 1], v_new], axis=1)
    taps = jnp.arange(span + 1)
    idx = L + jnp.arange(S)[:, None] - taps[None, :] * dil
    valid = idx >= 0
    idx = jnp.maximum(idx, 0)
    kg, vg = keys[:, idx], vals[:, idx]
    s = jnp.einsum('bshe,bsthe->bhst', q, kg).astype(jnp.float32) * HD ** -0.5
    s = s - slopes[:, None, None] * (taps * dil).astype(jnp.float32)[None, None, :]
    s = jnp.where(valid[None, None], s, NEG)
    lse = jax.nn.logsumexp(s, axis=-1)
    p = jnp.exp(s - lse[..., None])
    o = jnp.einsum('bhst,bsthe->bshe', p.astype(vg.dtype), vg)
    return o, lse.transpose(0, 2, 1)

def shared_kv(x, kv_norm, w_kv):
    B, L = x.shape[:2]
    return (rmsnorm(x, kv_norm) @ w_kv).reshape(B, L, 2, N_HEADS_B, HEAD_DIM)

def mixer_b(h, kv, w_q, w_o, slopes, attend):
    B, L = h.shape[:2]
    q = (h @ w_q).reshape(B, L, N_HEADS_B, HEAD_DIM)
    outs, lses = [], []
    for g in range(N_GROUPS_B):
        sl = slice(g * HPG, (g + 1) * HPG)
        o, lse = attend(g, q[:, :, sl], kv[:, :, 0, sl], kv[:, :, 1, sl], slopes[sl])
        outs.append(o)
        lses.append(lse)
    alpha = jax.nn.softmax(jnp.stack(lses, axis=0), axis=0)
    merged = jnp.concatenate([o * alpha[g][..., None].astype(o.dtype) for g, o in enumerate(outs)], axis=2)
    return merged.reshape(B, L, ATT_W) @ w_o

def trunk(x, attend, p):
    slopes = alibi_slopes()
    a_rows = []
    kv = None
    for layer in range(DEPTH):
        if layer < N_A_LAYERS:
            i = layer
            mix, rows = mixer_a(rmsnorm(x, p['a_norm'][i]), p['a_w_in'][i], p['a_v_norm'][i],
                                p['a_w_s'][i], p['a_b_s'][i], p['a_w_out'][i])
            a_rows.append(rows)
        else:
            if kv is None:
                kv = shared_kv(x, p['kv_norm'], p['w_kv'])
            j = layer - N_A_LAYERS
            mix = mixer_b(rmsnorm(x, p['b_norm'][j]), kv, p['b_w_q'][j], p['b_w_o'][j], slopes, attend)
        x = x + mix
        x = x + peer(rmsnorm(x, p['ffn_norm'][layer]), p['peer_w_q'][layer], p['peer_sub_keys'][layer],
                     p['peer_u'][layer], p['peer_v'][layer])
    return rmsnorm(x, p['final_norm']), jnp.stack(a_rows, axis=0), kv

def window_rows(kv):
    T = kv.shape[1]
    return [kv[:, T - min(w, T):, :, g * HPG:(g + 1) * HPG] for g, w in enumerate(WINDOWS)]

def setup_inputs(seed: int = 0) -> dict:
    key = jax.random.key(seed)
    ks = jax.random.split(key, 24)
    f32 = jnp.float32

    def nrm(k, shape, scale):
        return jax.random.normal(k, shape, f32) * scale

    def gain(k, shape):
        return 1.0 + 0.05 * jax.random.normal(k, shape, f32)

    lens = [min(w, PAST_LEN) for w in WINDOWS]
    return {
        'x_prompt': nrm(ks[0], (BATCH, SEQ, D_MODEL), 1.0),
        'x_sample': nrm(ks[1], (DEC_BATCH, DEC_SEQ, D_MODEL), 1.0),
        'cache_kv_w128': nrm(ks[2], (DEC_BATCH, lens[0], 2, HPG, HEAD_DIM), 1.0),
        'cache_kv_w512': nrm(ks[3], (DEC_BATCH, lens[1], 2, HPG, HEAD_DIM), 1.0),
        'cache_kv_w2048': nrm(ks[4], (DEC_BATCH, lens[2], 2, HPG, HEAD_DIM), 1.0),
        'a_norm': gain(ks[5], (N_A_LAYERS, D_MODEL)),
        'a_w_in': nrm(ks[6], (N_A_LAYERS, D_MODEL, 2 * D_AV), D_MODEL ** -0.5),
        'a_v_norm': gain(ks[7], (N_A_LAYERS, D_AV)),
        'a_w_s': nrm(ks[8], (N_A_LAYERS, A_GROUPS, CHUNK, CHUNK), 0.5 * CHUNK ** -0.5),
        'a_b_s': 1.0 + 0.1 * jax.random.normal(ks[9], (N_A_LAYERS, A_GROUPS, CHUNK), f32),
        'a_w_out': nrm(ks[10], (N_A_LAYERS, D_AV, D_MODEL), D_AV ** -0.5),
        'kv_norm': gain(ks[11], (D_MODEL,)),
        'w_kv': nrm(ks[12], (D_MODEL, 2 * ATT_W), D_MODEL ** -0.5),
        'b_norm': gain(ks[13], (N_B_LAYERS, D_MODEL)),
        'b_w_q': nrm(ks[14], (N_B_LAYERS, D_MODEL, ATT_W), D_MODEL ** -0.5),
        'b_w_o': nrm(ks[15], (N_B_LAYERS, ATT_W, D_MODEL), ATT_W ** -0.5),
        'ffn_norm': gain(ks[16], (DEPTH, D_MODEL)),
        'peer_w_q': nrm(ks[17], (DEPTH, D_MODEL, PEER_HEADS * D_QUERY), D_MODEL ** -0.5),
        'peer_sub_keys': nrm(ks[18], (DEPTH, 2, N_KEYS, D_HALF), D_HALF ** -0.5),
        'peer_u': nrm(ks[19], (DEPTH, N_EXPERTS, D_MODEL), D_MODEL ** -0.5),
        'peer_v': nrm(ks[20], (DEPTH, N_EXPERTS, D_MODEL), PEER_HEADS ** -0.5),
        'final_norm': gain(ks[21], (D_MODEL,)),
    }

def reference(x_prompt, x_sample, cache_kv_w128, cache_kv_w512, cache_kv_w2048,
              a_norm, a_w_in, a_v_norm, a_w_s, a_b_s, a_w_out,
              kv_norm, w_kv, b_norm, b_w_q, b_w_o,
              ffn_norm, peer_w_q, peer_sub_keys, peer_u, peer_v, final_norm):
    p = dict(a_norm=a_norm, a_w_in=a_w_in, a_v_norm=a_v_norm, a_w_s=a_w_s, a_b_s=a_b_s, a_w_out=a_w_out,
             kv_norm=kv_norm, w_kv=w_kv, b_norm=b_norm, b_w_q=b_w_q, b_w_o=b_w_o,
             ffn_norm=ffn_norm, peer_w_q=peer_w_q, peer_sub_keys=peer_sub_keys,
             peer_u=peer_u, peer_v=peer_v, final_norm=final_norm)
    caches = (cache_kv_w128, cache_kv_w512, cache_kv_w2048)

    def attend_prompt(g, q, k, v, sl):
        return dilated_attn_prompt(q, k, v, WINDOWS[g], DILATIONS[g], sl)

    def attend_sample(g, q, k, v, sl):
        return dilated_attn_sample(q, k, v, caches[g], WINDOWS[g], DILATIONS[g], sl)

    y_prompt, a_v_prompt, kv_p = trunk(x_prompt, attend_prompt, p)
    y_sample, a_v_sample, kv_s = trunk(x_sample, attend_sample, p)
    kv_w128_prompt, kv_w512_prompt, kv_w2048_prompt = window_rows(kv_p)
    kv_w128_sample, kv_w512_sample, kv_w2048_sample = window_rows(kv_s)
    return (y_prompt, y_sample, a_v_prompt, a_v_sample,
            kv_w128_prompt, kv_w512_prompt, kv_w2048_prompt,
            kv_w128_sample, kv_w512_sample, kv_w2048_sample)


_drawn_inputs = setup_inputs


def setup_inputs(seed=0):
    import zlib

    import numpy as np

    out = dict(_drawn_inputs(seed))
    spreads = {}
    factors = {'b_norm': 3.868}
    for name, (base, spread) in spreads.items():
        noise = np.random.default_rng([zlib.crc32(name.encode()), seed]).standard_normal(out[name].shape)
        drawn = base * np.exp(spread * noise) if base else spread * noise
        out[name] = __import__('jax').numpy.asarray(drawn.astype(out[name].dtype))
    for name, factor in factors.items():
        out[name] = (out[name] * factor).astype(out[name].dtype)
    return out
```

```python
from contextlib import ExitStack

import numpy as np

import concourse.bass as bass
from concourse import mybir

F32 = mybir.dt.float32
BF16 = mybir.dt.bfloat16
U32 = mybir.dt.uint32
ACT = mybir.ActivationFunctionType
ALU = mybir.AluOpType
AXX = mybir.AxisListType.X

P = 128
D = 1024
DC = D // P
NPROMPT, NB, NS = 256, 8, 4
NSAMP = NB * NS
T = NPROMPT + NSAMP
TILES = [(0, 128), (128, 128), (256, 32)]
EPS = 1e-6
DAV = 2 * D
FC = DAV // P
AG = 8
HP = 16
PH = 8
TOP = 16
NK = 128
NQ = 4
EQ = NK // NQ
GT = 8
NGG = T // GT
ROUNDS = 2
HALF = NGG // ROUNDS
LEAD = 2
RH = 3
CREDIT = 3
NG, HPG, HD = 3, 4, 64
WINDOWS = (128, 512, 2048)
DILS = (1, 4, 16)
NHB = NG * HPG
AW = NHB * HD
AC = AW // P
PAST = 1024
SLOPES = [float(np.float32(2.0 ** (-8.0 * (i + 1) / NHB))) for i in range(NHB)]
CK = [128, 128, 64]
CS = [1, 4, 4]
COFF = [0, 256, 1280]
KV = 2304
SCOLS = sum(CK) + NG * NSAMP
BLK = 2048
R = 4
BIG = -3.0e38

TO_ACT = [("u", FC), ("v", 12), ("q0", HP), ("s0", 12), ("U0", NK),
          ("k", AC), ("vn", 9), ("qb", AC), ("qn", 2), ("sp", 2), ("so", 1), ("pp", 20),
          ("q1", HP), ("s1", 12), ("U1", NK)]
TO_DVE = [("na", 1), ("gate", FC), ("wo", DC), ("n0", 1), ("e0", 3), ("V0", NQ * DC),
          ("nb", 1), ("qk", 48), ("sc", 3), ("ps", 24), ("ob", DC), ("n1", 1), ("e1", 3),
          ("V1", NQ * DC), ("nf", 1)]


def due(done, of):
    return done * HALF // of


def starts(stages):
    at, out = 0, {}
    for name, n in stages:
        out[name] = at
        at += n
    return out


def build(nc, i, o):
    A0, D0 = starts(TO_ACT), starts(TO_DVE)
    with ExitStack() as ctx:
        def sb(name, shape, dt=F32):
            return ctx.enter_context(nc.sbuf_tensor(name, shape, dt))

        def sem(name):
            return ctx.enter_context(nc.semaphore(name))

        xT = sb("xT", [P, DC, T])
        hT = sb("hT", [P, DC, T])
        rs = sb("rs", [P, 3, T])
        stat = sb("stat", [P, 16])
        ring = sb("ring", [P, R, BLK])
        wide = sb("wide", [P, 16 * T])
        mid = sb("mid", [P, 3 * DAV])
        big = sb("big", [P, 2 * EQ * T])
        work = sb("work", [P, 5632])
        slots = sb("slots", [P, 3, 3 * P])
        halves = sb("halves", [P, 2, 3 * P], BF16)
        parts = sb("parts", [P, 3, 3 * P], BF16)
        iota16 = sb("iota16", [P, NK], BF16)
        ident = sb("ident", [P, P])
        iota = sb("iota", [P, P])
        ones = sb("ones", [P, P])
        gains = sb("gains", [P, 6, DC])
        skT = sb("skT", [P, 2, 2, NK])
        sbias = sb("sbias", [P, SCOLS])
        ps = ctx.enter_context(nc.psum_tensor("ps", [P, 8, 512], F32))

        def view(t, at, *shape, parts=P):
            n = int(np.prod(shape))
            v = t[0:parts, at:at + n]
            if len(shape) == 1:
                return v
            names = "abcd"[:len(shape)]
            return v.rearrange(f"p ({' '.join(names)}) -> p {' '.join(names)}",
                               **{c: s for c, s in zip(names, shape)})

        uT = view(wide, 0, FC, T)
        v = view(mid, 0, 3, DAV)
        vgain = view(big, 0, DAV)
        bsp = view(big, DAV, AG, P)
        bss = view(big, DAV + AG * P, AG, NSAMP)
        wsp = view(big, 3328, AG, P)
        wss = view(big, 4352, AG, NSAMP)
        maskp = view(big, 4608, P)
        masks = view(big, 4736, NSAMP)
        qT = view(wide, 0, HP, T)
        S3 = view(mid, 0, 3, HP * NK)
        S = view(big, EQ * T, HP, NK)
        cand = view(big, EQ * T + 2048, PH, TOP * TOP)
        eq = view(big, EQ * T + 4096, PH * TOP, TOP)
        tv = view(work, 0, HP, TOP)
        ti = work[:, 256:512].bitcast(U32).rearrange("p (a b) -> p a b", a=HP)
        tif = view(work, 512, PH, 2, TOP)
        cs = view(work, 768, PH, TOP)
        pos = work[:, 896:1024].bitcast(U32)
        pos12 = work[:, 1024:1280].bitcast(U32).rearrange("p (a b) -> p a b", a=2)
        posf = view(work, 1280, 2, PH * TOP)
        gs = view(work, 1536, 3 * PH, TOP)
        gsum = view(work, 1920, 3 * PH)
        grec = view(work, 1944, 3 * PH)
        eg = view(work, 1968, 3, 3, P)
        hot1 = work[:, 0:1536].bitcast(BF16).rearrange("p (r t e) -> p r t e", r=RH, t=GT)
        hot2 = work[:, 1536:2688].bitcast(BF16).rearrange("p (r c t e) -> p r c t e", r=RH, c=3, t=GT)
        here2 = work[:, 2688:3072].bitcast(BF16).rearrange("p (r t e) -> p r t e", r=RH, t=GT)
        C = view(big, 0, 2, EQ, T)
        aq = view(wide, 0, AC, T)
        ak = view(wide, AC * T, AC, T)
        Sk = view(wide, 2 * AC * T, NG, P)
        Ss = view(wide, 2 * AC * T + 384, SCOLS)
        av = view(mid, 0, 3, AW)
        dist = view(mid, 2304, NG, 2, 256)
        Pp = view(mid, 3840, NG, 256)
        PpT = view(mid, 4608, 6, P)
        PsT = view(mid, 5376, 6, P)
        Vc = view(big, 0, NB, KV)
        Kc = view(work, 0, 2, KV)
        prod = view(work, 2 * KV, 16, HD)
        qn = slots[0:NSAMP].rearrange("p a b -> p (a b)")[:, 0:AW]

        landed = [sem(f"landed{r}") for r in range(R)]
        blocks_begun = sem("blocks_begun")
        x_loaded, consts_loaded, mix_loaded = sem("x_loaded"), sem("consts_loaded"), sem("mix_loaded")
        act_full, act_free = sem("act_full"), sem("act_free")
        dve_full, dve_free = sem("dve_full"), sem("dve_free")
        ones_set = sem("ones_set")
        x_ready = sem("x_ready")
        squares = sem("squares")
        ms_ready, root_ready = sem("ms_ready"), sem("root_ready")
        h_ready = sem("h_ready")
        v_square, v_ready, ws_ready, ug_ready = sem("v_square"), sem("v_ready"), sem("ws_ready"), sem("ug_ready")
        exp_in, exp_out = sem("exp_in"), sem("exp_out")
        slot_ready = sem("slot_ready")
        hot_ready = sem("hot_ready")
        gate_full, gate_free = sem("gate_full"), sem("gate_free")
        dstep = sem("dstep")
        vc_loaded, dist_loaded = sem("vc_loaded"), sem("dist_loaded")
        k_landed = [sem("k_landed0"), sem("k_landed1")]
        k_used = sem("k_used")
        sm_in, sm_exp, sm_out = sem("sm_in"), sem("sm_exp"), sem("sm_out")
        pp_in, pp_exp, pp_out = sem("pp_in"), sem("pp_exp"), sem("pp_out")
        moved = sem("moved")
        av_saved, kv_saved, out_done = sem("av_saved"), sem("kv_saved"), sem("out_done")

        block = ctx.enter_context(nc.Block())

        @block.sync
        def _(sp):
            sp.dma_start(xT[:], i["xT"]).then_inc(x_loaded, 16)
            n = 0
            for name in ("w_in_u", "w_in_v", "w_out", "peer_q0", "U0", "V0", "w_k", "w_v", "w_q",
                         "w_o", "peer_q1", "U1", "V1"):
                if name.startswith("V"):
                    continue
                src = i[name]
                if name.startswith("U"):
                    vsrc = i["V" + name[1]]
                    per = 64 // NQ
                    order = [(src, 0), (src, per)]
                    for q in range(NQ):
                        order.append((vsrc, q * per))
                        if q + 2 < NQ:
                            order.append((src, (q + 2) * per))
                    for s, b0 in order:
                        with sp.Fori(0, per // R) as it:
                            for r in range(R):
                                sp.wait_ge(blocks_begun, it * R + (n + r - R + 2))
                                sp.dma_start(ring[:, r, :], s[it * R + (b0 + r)]).then_inc(landed[r], 16)
                        n += per
                    continue
                for b in range(src.shape[0]):
                    if n >= R:
                        sp.wait_ge(blocks_begun, n - R + 2)
                    sp.dma_start(ring[:, n % R, :], src[b]).then_inc(landed[n % R], 16)
                    n += 1

        @block.gpsimd
        def _(pool):
            pool.memset(ones[:], 1.0)
            pool.memset(S3[:, 2, :], 0.0).then_inc(ones_set, 1)
            for t, s in ((ident[:], "ident"), (iota[:], "iota"), (gains[:], "gains"),
                         (skT[:], "skT"), (sbias[:], "sbias")):
                pool.dma_start(t, i[s]).then_inc(consts_loaded, 16)
            pool.dma_start(vgain, i["vgain"].partition_broadcast(P)).then_inc(mix_loaded, 16)
            pool.dma_start(bsp, i["bsp"].partition_broadcast(P)).then_inc(mix_loaded, 16)
            pool.dma_start(bss, i["bss"].partition_broadcast(P)).then_inc(mix_loaded, 16)
            pool.dma_start(wsp, i["wsp"]).then_inc(mix_loaded, 16)
            pool.dma_start(wss[0:NSAMP], i["wss"]).then_inc(mix_loaded, 16)
            pool.dma_start(maskp, i["maskp"]).then_inc(mix_loaded, 16)
            pool.dma_start(masks[0:NSAMP], i["masks"]).then_inc(mix_loaded, 16)
            pool.wait_ge(v_ready, 1)
            pool.dma_start(o["a_v_prompt"], v[:, 1, :]).then_inc(av_saved, 16)
            pool.dma_start(o["a_v_sample"], v[0:NSAMP, 2, :]).then_inc(av_saved, 16)
            pool.wait_ge(x_ready, 2)
            pool.dma_start(dist, i["dist"]).then_inc(dist_loaded, 16)
            cache = [i["cache0"], i["cache1"], i["cache2"]]

            def load_cache(dst, b, which, done):
                for g in range(NG):
                    n, s = CK[g], CS[g]
                    rows = cache[g][b].rearrange("(r s) k c -> r s k c", r=n)[:, 0:s, which, :]
                    d = dst[0:n, COFF[g]:COFF[g] + s * 256].rearrange("p (s c) -> p s c", s=s)
                    pool.dma_start(d, rows).then_inc(done, 16)

            for b in range(NB):
                if b >= 2:
                    pool.wait_ge(k_used, b - 1)
                load_cache(Kc[:, b % 2, :], b, 0, k_landed[b % 2])
                load_cache(Vc[:, b, :], b, 1, vc_loaded)
            pool.wait_ge(act_free, A0["qn"])
            pool.dma_start(o["kT"], ak).then_inc(kv_saved, 16)
            pool.dma_start(o["v_prompt"], av[:, 0:2, :]).then_inc(kv_saved, 16)
            pool.dma_start(o["v_sample"], av[0:NSAMP, 2, :]).then_inc(kv_saved, 16)
            pool.wait_ge(h_ready, 6)
            pool.dma_start(o["yT"], hT[:]).then_inc(out_done, 16)
            pool.wait_ge(av_saved, 16 * 2)
            pool.wait_ge(kv_saved, 16 * 3)
            pool.wait_ge(out_done, 16)

        @block.tensor
        def _(pe):
            state = {"block": 0}

            def arrived(n, i4=None, rounds=0):
                want = 16 * (n // R + 1)
                pe.wait_ge(landed[n % R], want if i4 is None else i4 * (16 * rounds) + want)
                return n % R

            def act_bank(stage, k):
                if k < 4:
                    if A0[stage] > 0:
                        pe.wait_ge(act_free, A0[stage])
                else:
                    pe.wait_ge(act_free, A0[stage] + k - 3)
                return k % 4

            def dve_bank(stage, k):
                if k < 4:
                    if D0[stage] > 0:
                        pe.wait_ge(dve_free, D0[stage])
                else:
                    pe.wait_ge(dve_free, D0[stage] + k - 3)
                return 4 + k % 4

            def mean_square(stage, nth):
                pe.wait_ge(squares, nth)
                b = dve_bank(stage, 0)
                for c in range(DC):
                    last = pe.matmul(ps[:, b, 0:T], ones[:], hT[:, c, :], start=(c == 0), stop=(c == DC - 1))
                last.then_inc(dve_full, 1)

            def project(stage, nblocks):
                for bl in range(nblocks):
                    r = arrived(state["block"])
                    for j in range(2):
                        b = act_bank(stage, 2 * bl + j)
                        for c in range(DC):
                            at = (j * DC + c) * P
                            last = pe.matmul(ps[:, b, 0:T], ring[:, r, at:at + P], hT[:, c, :],
                                             start=(c == 0), stop=(c == DC - 1))
                            if c == 0 and j == 0:
                                last.then_inc(blocks_begun, 1)
                        last.then_inc(act_full, 1)
                    state["block"] += 1

            pe.wait_ge(ones_set, 1)
            mean_square("na", 1)
            pe.wait_ge(h_ready, 1)
            project("u", 8)
            for fg in range(4):
                n0 = state["block"]
                rr = [arrived(n0), arrived(n0 + 1)]
                for m, (t0, tn) in enumerate(TILES):
                    b = act_bank("v", 3 * fg + m)
                    for c in range(DC):
                        last = pe.matmul(ps[0:tn, b, :], hT[:, c, t0:t0 + tn],
                                         ring[:, rr[c // 4], (c % 4) * 512:(c % 4 + 1) * 512],
                                         start=(c == 0), stop=(c == DC - 1))
                        if (m, c) in ((0, 0), (2, 4)):
                            last.then_inc(blocks_begun, 1)
                    last.then_inc(act_full, 1)
                state["block"] += 2
            pe.wait_ge(v_ready, 1)
            pe.wait_ge(ws_ready, 1)
            for c in range(FC):
                b = dve_bank("gate", c)
                g = c * P // 256
                for m, (t0, tn) in enumerate(TILES):
                    w = wsp[:, g, :] if m < 2 else wss[0:NSAMP, g, :]
                    last = pe.matmul(ps[:, b, t0:t0 + tn], v[0:tn, m, c * P:(c + 1) * P], w, start=True, stop=True)
                last.then_inc(dve_full, 1)
            for c in range(DC):
                r = arrived(state["block"])
                b = dve_bank("wo", c)
                for f in range(FC):
                    if c == 0:
                        pe.wait_ge(ug_ready, f + 1)
                    last = pe.matmul(ps[:, b, 0:T], ring[:, r, f * P:(f + 1) * P], uT[:, f, :],
                                     start=(f == 0), stop=(f == FC - 1))
                    if f == 0:
                        last.then_inc(blocks_begun, 1)
                last.then_inc(dve_full, 1)
                state["block"] += 1

            def peer(layer):
                mean_square(f"n{layer}", 2 + 2 * layer)
                pe.wait_ge(h_ready, 2 + 3 * layer)
                project(f"q{layer}", 8)
                pe.wait_ge(act_free, A0[f"s{layer}"])
                for m, (t0, tn) in enumerate(TILES):
                    for g4 in range(4):
                        b = act_bank(f"s{layer}", 4 * m + g4)
                        for j in range(4):
                            hp = 4 * g4 + j
                            last = pe.matmul(ps[0:tn, b, j * NK:(j + 1) * NK], qT[:, hp, t0:t0 + tn],
                                             skT[:, layer, hp % 2, :], start=True, stop=True)
                        last.then_inc(act_full, 1)

                def slot_transposes():
                    for m in range(3):
                        pe.wait_ge(slot_ready, layer + 1)
                        b = dve_bank(f"e{layer}", m)
                        for a in range(3):
                            last = pe.transpose(ps[:, b, a * P:(a + 1) * P], eg[:, m, a, :], ident[:])
                        last.then_inc(dve_full, 1)

                def gate_groups(q, done, of, it):
                    if q is None:
                        return
                    nth = layer * NQ + q
                    for j in range(due(done, of), due(done + 1, of)):
                        pe.wait_ge(hot_ready, it * HALF + (nth * (NGG + LEAD) + j + 1))
                        pe.wait_ge(gate_free, it * HALF + (nth * NGG + j - 1 + CREDIT))
                        for t in range(GT):
                            for c in range(3):
                                g = pe.matmul(ps[:, 6 + j % 2, t * EQ:(t + 1) * EQ], hot1[:, j % RH, t, :],
                                              hot2[:, j % RH, c, t, :], start=(c == 0), stop=(c == 2))
                        g.then_inc(gate_full, 1)

                def up(q, gq=None):
                    n0 = state["block"]
                    k0 = A0[f"U{layer}"] + q * EQ
                    with pe.Fori(0, 2) as it:
                        for bl in range(8):
                            r = arrived(n0 + bl, it, 2)
                            for j in range(2 * bl, 2 * bl + 2):
                                pe.wait_ge(act_free, it * 16 + (k0 + j - 3))
                                for c in range(DC):
                                    at = ((j % 2) * DC + c) * P
                                    last = pe.matmul(ps[:, j % 4, 0:T], ring[:, r, at:at + P], hT[:, c, :],
                                                     start=(c == 0), stop=(c == DC - 1))
                                    if c == 0 and j % 2 == 0:
                                        last.then_inc(blocks_begun, 1)
                                    if c == DC - 1:
                                        last.then_inc(act_full, 1)
                                    gate_groups(gq, j * DC + c, 16 * DC, it)
                    state["block"] += EQ // 2

                def down(q, gq=None):
                    n0 = state["block"]
                    k0 = D0[f"V{layer}"] + q * DC
                    pe.wait_ge(gate_free, (layer * NQ + q + 1) * NGG + CREDIT)
                    with pe.Fori(0, 2) as it:
                        for bl in range(8):
                            dc, hb = bl // 2, bl % 2
                            if hb == 0:
                                pe.wait_ge(dve_free, it * 4 + (k0 + dc - 1))
                            r = arrived(n0 + bl, it, 2)
                            for e in range(16):
                                last = pe.matmul(ps[:, 4 + dc % 2, 0:T], ring[:, r, e * P:(e + 1) * P],
                                                 C[:, q % 2, hb * 16 + e, :],
                                                 start=(hb == 0 and e == 0), stop=(hb == 1 and e == 15))
                                if e == 0:
                                    last.then_inc(blocks_begun, 1)
                                if hb == 1 and e == 15:
                                    last.then_inc(dve_full, 1)
                                gate_groups(gq, bl * 16 + e, 128, it)
                    state["block"] += 16

                up(0)
                slot_transposes()
                pe.wait_ge(dve_free, D0[f"V{layer}"])
                up(1, 0)
                for q in range(NQ):
                    down(q, q + 1 if q + 1 < NQ else None)
                    if q + 2 < NQ:
                        up(q + 2)

            peer(0)

            mean_square("nb", 3)
            pe.wait_ge(h_ready, 3)
            project("k", 3)
            for fg in range(3):
                r = arrived(state["block"])
                for m, (t0, tn) in enumerate(TILES):
                    b = act_bank("vn", 3 * fg + m)
                    for c in range(DC):
                        last = pe.matmul(ps[0:tn, b, 0:256], hT[:, c, t0:t0 + tn], ring[:, r, c * 256:(c + 1) * 256],
                                         start=(c == 0), stop=(c == DC - 1))
                        if m == 0 and c == 0:
                            last.then_inc(blocks_begun, 1)
                    last.then_inc(act_full, 1)
                state["block"] += 1
            pe.wait_ge(h_ready, 4)
            project("qb", 3)
            for k in range(2):
                b = act_bank("qn", k)
                for j in range(3):
                    last = pe.transpose(ps[0:NSAMP, b, j * P:(j + 1) * P], aq[:, 3 * k + j, NPROMPT:T], ident[:])
                last.then_inc(act_full, 1)
            pe.wait_ge(act_free, A0["sp"])
            for b_ in range(NB):
                for g in range(NG):
                    for pr in range(2):
                        b = dve_bank("qk", (b_ * NG + g) * 2 + pr)
                        for j in range(2):
                            tok = NS * b_ + 2 * pr + j
                            last = pe.matmul(ps[:, b, j * 256:(j + 1) * 256],
                                             ident[0:NSAMP, tok:tok + 1].broadcast_to((NSAMP, P)),
                                             qn[:, g * 256:(g + 1) * 256], start=True, stop=True)
                        last.then_inc(dve_full, 1)
            pe.wait_ge(k_used, NB)
            b = dve_bank("sc", 0)
            at = 0
            for g in range(NG):
                last = pe.transpose(ps[:, b, at:at + CK[g]], Sk[0:CK[g], g, :], ident[0:CK[g], 0:CK[g]])
                at += CK[g]
            last.then_inc(dve_full, 1)
            for par in range(2):
                b = dve_bank("sc", 1 + par)
                for h in (par, par + 2):
                    for g in range(NG):
                        row = par * HD
                        last = pe.matmul(ps[32 * h:32 * h + 32, b, g * NSAMP:(g + 1) * NSAMP],
                                         aq[row:row + HD, 2 * g + h // 2, NPROMPT:T],
                                         ak[row:row + HD, 2 * g + h // 2, NPROMPT:T], start=True, stop=True)
                last.then_inc(dve_full, 1)

            def prompt_scores(u):
                h, m = u // 2, u % 2
                row = (h % 2) * HD
                for g in range(NG):
                    b = dve_bank("ps", 3 * u + g)
                    pe.matmul(ps[:, b, 0:P * (m + 1)], aq[row:row + HD, 2 * g + h // 2, m * P:(m + 1) * P],
                              ak[row:row + HD, 2 * g + h // 2, 0:P * (m + 1)],
                              start=True, stop=True).then_inc(dve_full, 1)

            pe.wait_ge(sm_out, 1)
            b = act_bank("sp", 0)
            at = 0
            for g in range(NG):
                last = pe.transpose(ps[0:CK[g], b, g * P:(g + 1) * P], Ss[:, at:at + CK[g]], ident[:])
                at += CK[g]
            last.then_inc(act_full, 1)
            b = act_bank("sp", 1)
            for g in range(NG):
                last = pe.transpose(ps[0:NSAMP, b, g * P:(g + 1) * P], Ss[:, at:at + NSAMP], ident[:])
                at += NSAMP
            last.then_inc(act_full, 1)
            pe.wait_ge(vc_loaded, 16 * NG * NB)
            b = act_bank("so", 0)
            for g in range(NG):
                for pr in range(2):
                    dst = ps[:, b, (g * 2 + pr) * 64:(g * 2 + pr + 1) * 64]
                    dst3 = dst.rearrange("p (j t) -> p j t", j=2)
                    pe.matmul(dst, av[0:NSAMP, 2, g * 256 + pr * P:g * 256 + (pr + 1) * P],
                              PsT[0:NSAMP, 3 + g, pr * 64:(pr + 1) * 64], start=True, stop=False,
                              skip_group_check=True)
                    prob = PsT[0:CK[g], g, pr * 64:(pr + 1) * 64].rearrange("p (j t) -> p j t", j=2)
                    for b_ in range(NB):
                        for s in range(CS[g]):
                            w = NS // CS[g]
                            t0 = NS * b_ + s * w
                            at = COFF[g] + s * 256 + pr * P
                            last = pe.matmul(dst3[:, :, t0:t0 + w], Vc[0:CK[g], b_, at:at + P],
                                             prob[:, :, t0:t0 + w], start=False,
                                             stop=(b_ == NB - 1 and s == CS[g] - 1), skip_group_check=True)
            last.then_inc(act_full, 1)

            prompt_scores(0)
            kk = 0
            for u in range(8):
                h, m = u // 2, u % 2
                if u + 1 < 8:
                    prompt_scores(u + 1)
                pe.wait_ge(pp_out, u + 1)
                for half in range(m + 1):
                    b = act_bank("pp", kk)
                    kk += 1
                    for g in range(NG):
                        last = pe.transpose(ps[:, b, g * P:(g + 1) * P], Pp[:, g, half * P:(half + 1) * P], ident[:])
                    last.then_inc(act_full, 1)
                b = act_bank("pp", kk)
                pe.wait_ge(act_free, A0["pp"] + kk)
                kk += 1
                row = (h % 2) * HD
                for g in range(NG):
                    f0 = g * 256 + h * HD
                    for half in range(m + 1):
                        last = pe.matmul(ps[row:row + HD, b, g * P:(g + 1) * P], av[:, half, f0:f0 + HD],
                                         PpT[:, half * 3 + g, :], start=(half == 0), stop=(half == m))
                last.then_inc(act_full, 1)
            pe.wait_ge(act_free, A0["q1"])
            for c in range(DC):
                b = dve_bank("ob", c)
                for f in range(AC):
                    k = c * AC + f
                    if k % 16 == 0:
                        r = arrived(state["block"])
                    last = pe.matmul(ps[:, b, 0:T], ring[:, r, (k % 16) * P:(k % 16 + 1) * P], hT[:, f, :],
                                     start=(f == 0), stop=(f == AC - 1))
                    if k % 16 == 0:
                        last.then_inc(blocks_begun, 1)
                        state["block"] += 1
                last.then_inc(dve_full, 1)
            peer(1)
            mean_square("nf", 5)

        @block.scalar
        def _(act):
            def full(stage, k):
                act.wait_ge(act_full, A0[stage] + k + 1)
                return k % 4

            def norm_part(nth):
                act.wait_ge(x_ready, nth - 1) if nth > 1 else act.wait_ge(x_loaded, 16)
                act.activation(hT[:], xT[:], ACT.Square).then_inc(squares, 1)
                act.wait_ge(ms_ready, nth if nth == 1 else nth + 1)
                act.activation(rs[:, 1, :], rs[:, 0, :], ACT.Sqrt).then_inc(root_ready, 1)

            act.wait_ge(ones_set, 1)
            norm_part(1)
            for c in range(FC):
                b = full("u", c)
                act.activation(uT[:, c, :], ps[:, b, 0:T], ACT.Gelu_apprx_tanh).then_inc(act_free, 1)
            for fg in range(4):
                for m, (t0, tn) in enumerate(TILES):
                    b = full("v", 3 * fg + m)
                    act.activation(v[0:tn, m, fg * 512:(fg + 1) * 512], ps[0:tn, b, :],
                                   ACT.Gelu_apprx_tanh).then_inc(act_free, 1)
            act.wait_ge(act_free, A0["q0"])
            act.wait_ge(moved, 1)
            for m, (t0, tn) in enumerate(TILES):
                junk = work[0:tn, m * DAV:(m + 1) * DAV] if m < 2 else view(hT.rearrange("p a b -> p (a b)"), 0, DAV, parts=tn)
                last = act.activation(junk, v[0:tn, m, :], ACT.Square, accum_out=stat[0:tn, m:m + 1])
            last.then_inc(v_square, 1)
            act.wait_ge(ms_ready, 2)
            act.activation(stat[:, 6:9], stat[:, 3:6], ACT.Sqrt).then_inc(root_ready, 1)

            def peer(layer):
                norm_part(2 + 2 * layer)
                if layer == 1:
                    act.wait_ge(kv_saved, 16 * 3)
                for c in range(HP):
                    b = full(f"q{layer}", c)
                    act.activation(qT[:, c, :], ps[:, b, 0:T], ACT.Copy).then_inc(act_free, 1)

                def up(q):
                    k0 = A0[f"U{layer}"] + q * EQ
                    with act.Fori(0, EQ // 8) as it:
                        for j in range(8):
                            act.wait_ge(act_full, it * 8 + (k0 + j + 1))
                            act.activation(C[:, q % 2, it * 8 + j, :], ps[:, j % 4, 0:T],
                                           ACT.Gelu_apprx_tanh).then_inc(act_free, 1)

                if layer == 0:
                    act.wait_ge(av_saved, 16 * 2)
                for m, (t0, tn) in enumerate(TILES):
                    for g4 in range(4):
                        b = full(f"s{layer}", 4 * m + g4)
                        act.activation(S3[0:tn, m, g4 * 512:(g4 + 1) * 512], ps[0:tn, b, :], ACT.Copy).then_inc(act_free, 1)
                up(0)
                act.wait_ge(exp_in, layer + 1)
                act.activation(gs, gs, ACT.Exp).then_inc(exp_out, 1)
                for q in range(1, NQ):
                    up(q)

            peer(0)

            norm_part(3)
            for c in range(AC):
                b = full("k", c)
                act.activation(ak[:, c, :], ps[:, b, 0:T], ACT.Copy).then_inc(act_free, 1)
            for fg in range(3):
                for m, (t0, tn) in enumerate(TILES):
                    b = full("vn", 3 * fg + m)
                    act.activation(av[0:tn, m, fg * 256:(fg + 1) * 256], ps[0:tn, b, 0:256],
                                   ACT.Copy).then_inc(act_free, 1)
            for c in range(AC):
                b = full("qb", c)
                act.activation(aq[:, c, :], ps[:, b, 0:T], ACT.Copy, scale=HD ** -0.5).then_inc(act_free, 1)
            for k in range(2):
                b = full("qn", k)
                act.activation(qn[:, k * 384:(k + 1) * 384], ps[0:NSAMP, b, 0:384], ACT.Copy).then_inc(act_free, 1)
            act.wait_ge(sm_in, 1)
            act.activation(Ss, Ss, ACT.Exp, bias=stat[:, 9:10], accum_out=stat[:, 10:11]).then_inc(sm_exp, 1)
            b = full("sp", 0)
            act.activation(PsT[:, 0:2, :].rearrange("p a b -> p (a b)"), ps[:, b, 0:256], ACT.Copy)
            act.activation(PsT[0:CK[2], 2, :], ps[0:CK[2], b, 256:384], ACT.Copy).then_inc(act_free, 1)
            b = full("sp", 1)
            act.activation(PsT[0:NSAMP, 3:6, :].rearrange("p a b -> p (a b)"), ps[0:NSAMP, b, 0:384],
                           ACT.Copy).then_inc(act_free, 1)
            b = full("so", 0)
            o3 = ps[:, b, 0:384].rearrange("p (c j t) -> p c j t", c=AC, j=2)
            act.activation(hT[0:HD, 0:AC, NPROMPT:T], o3[0:HD, :, 0, :], ACT.Copy)
            act.activation(hT[HD:P, 0:AC, NPROMPT:T], o3[HD:P, :, 1, :], ACT.Copy).then_inc(act_free, 1)
            kk = 0
            for u in range(8):
                h, m = u // 2, u % 2
                row = (h % 2) * HD
                act.wait_ge(pp_in, u + 1)
                act.activation(Pp[:, :, 0:P * (m + 1)], Pp[:, :, 0:P * (m + 1)], ACT.Exp,
                               bias=stat[:, 11:12], accum_out=stat[:, 12:13]).then_inc(pp_exp, 1)
                for half in range(m + 1):
                    b = full("pp", kk)
                    kk += 1
                    act.activation(PpT[:, 3 * half:3 * half + 3, :].rearrange("p a b -> p (a b)"),
                                   ps[:, b, 0:384], ACT.Copy).then_inc(act_free, 1)
                b = full("pp", kk)
                kk += 1
                dst = hT[row:row + HD, :, m * P:(m + 1) * P]
                for g in range(NG):
                    last = act.activation(dst[:, 2 * g + h // 2, :], ps[row:row + HD, b, g * P:(g + 1) * P], ACT.Copy)
                last.then_inc(act_free, 1)
            peer(1)
            norm_part(5)

        @block.vector
        def _(dve):
            count = {"n": 0, "it": None, "per": 0}

            def link(ins):
                count["n"] += 1
                ins.then_inc(dstep, 1)
                it = count["it"]
                dve.wait_ge(dstep, count["n"] if it is None else it * count["per"] + count["n"])

            def loop(n, per, body):
                n0 = count["n"]
                with dve.Fori(0, n) as it:
                    count["it"], count["per"] = it, per
                    body(it)
                assert count["n"] == n0 + per, (count["n"] - n0, per)
                count["it"], count["n"] = None, n0 + n * per

            def full(stage, k):
                dve.wait_ge(dve_full, D0[stage] + k + 1)
                return 4 + k % 4

            def newton(r, ms, tmp):
                link(dve.tensor_tensor(tmp, r, r, ALU.mult))
                link(dve.tensor_tensor(tmp, tmp, ms, ALU.mult))
                link(dve.tensor_scalar(tmp, tmp, -0.5, 1.5, ALU.mult, ALU.add))
                link(dve.tensor_tensor(r, r, tmp, ALU.mult))

            def norm(stage, nth_root, gain):
                b = full(stage, 0)
                dve.tensor_scalar(rs[:, 0, :], ps[:, b, 0:T], 1.0 / D, EPS, ALU.mult, ALU.add).then_inc(dve_free, 1)
                dve.wait_ge(dve_free, D0[stage] + 1)
                dve.engine_nop().then_inc(ms_ready, 1)
                dve.wait_ge(root_ready, nth_root)
                link(dve.reciprocal(rs[:, 2, :], rs[:, 1, :]))
                newton(rs[:, 2, :], rs[:, 0, :], rs[:, 1, :])
                scaled(gain)

            def scaled(gain):
                for c in range(DC):
                    last = dve.scalar_tensor_tensor(out=hT[:, c, :], in0=xT[:, c, :], scalar=gains[:, gain, c:c + 1],
                                                    in1=rs[:, 2, :], op0=ALU.mult, op1=ALU.mult)
                last.then_inc(h_ready, 1)

            def add_chunks(stage):
                for c in range(DC):
                    b = full(stage, c)
                    dve.tensor_tensor(xT[:, c, :], xT[:, c, :], ps[:, b, 0:T], ALU.add).then_inc(dve_free, 1)
                dve.wait_ge(dve_free, D0[stage] + DC)
                dve.engine_nop().then_inc(x_ready, 1)

            dve.memset(stat[:], 1.0).then_inc(moved, 1)
            dve.engine_nop().then_inc(gate_free, CREDIT)
            dve.wait_ge(consts_loaded, 16 * 5)
            dve.tensor_copy(iota16[:], iota[:])
            dve.wait_ge(x_loaded, 16)
            norm("na", 1, 0)
            dve.wait_ge(mix_loaded, 16 * 7)
            dve.tensor_tensor(wsp, wsp, maskp.unsqueeze(1).broadcast_to((P, AG, P)), ALU.mult)
            dve.tensor_tensor(wss[0:NSAMP], wss[0:NSAMP],
                              masks[0:NSAMP].unsqueeze(1).broadcast_to((NSAMP, AG, NSAMP)), ALU.mult).then_inc(ws_ready, 1)
            dve.wait_ge(v_square, 1)
            dve.tensor_scalar(stat[:, 3:6], stat[:, 0:3], 1.0 / DAV, EPS, ALU.mult, ALU.add).then_inc(ms_ready, 1)
            dve.wait_ge(root_ready, 2)
            link(dve.reciprocal(stat[:, 9:12], stat[:, 6:9]))
            newton(stat[:, 9:12], stat[:, 3:6], stat[:, 12:15])
            for m, (t0, tn) in enumerate(TILES):
                last = dve.scalar_tensor_tensor(out=v[0:tn, m, :], in0=v[0:tn, m, :], scalar=stat[0:tn, 9 + m:10 + m],
                                                in1=vgain[0:tn], op0=ALU.mult, op1=ALU.mult)
            last.then_inc(v_ready, 1)
            dve.wait_ge(act_free, FC)
            for c in range(FC):
                b = full("gate", c)
                g = c * P // 256
                dve.tensor_tensor(ps[:, b, 0:NPROMPT].rearrange("p (m t) -> p m t", m=2),
                                  ps[:, b, 0:NPROMPT].rearrange("p (m t) -> p m t", m=2),
                                  bsp[:, g:g + 1, :].broadcast_to((P, 2, P)), ALU.add)
                link(dve.tensor_tensor(ps[:, b, NPROMPT:T], ps[:, b, NPROMPT:T], bss[:, g, :], ALU.add))
                dve.tensor_tensor(uT[:, c, :], uT[:, c, :], ps[:, b, 0:T], ALU.mult).then_inc(dve_free, 1)
                dve.wait_ge(dve_free, D0["gate"] + c + 1)
                dve.engine_nop().then_inc(ug_ready, 1)
            add_chunks("wo")

            def peer(layer):
                norm(f"n{layer}", 3 + 2 * layer, 1 if layer == 0 else 4)

                def take_wait():
                    dve.memset(stat[:, 15:16], 0.0)

                def top16(val, idx, src, n):
                    take_wait()
                    for a in range(n):
                        last = dve.max(val[:, a, 0:8], src[:, a, :])
                    link(last)
                    take_wait()
                    for a in range(n):
                        dve.max_index(idx[:, a, 0:8], val[:, a, 0:8], src[:, a, :])
                    for a in range(n):
                        last = dve.match_replace(src[:, a, :], val[:, a, 0:8], src[:, a, :], BIG)
                    link(last)
                    take_wait()
                    for a in range(n):
                        last = dve.max(val[:, a, 8:16], src[:, a, :])
                    link(last)
                    take_wait()
                    for a in range(n):
                        last = dve.max_index(idx[:, a, 8:16], val[:, a, 8:16], src[:, a, :])
                    return last

                def route(m):
                    link(dve.tensor_copy(S.rearrange("p a b -> p (a b)").unsqueeze(1), S3[:, bass.ds(m, 1), :]))
                    link(top16(tv, ti, S, HP))
                    tv4 = tv.rearrange("p (h s) k -> p h s k", s=2)
                    link(dve.tensor_tensor(cand.rearrange("p h (a b) -> p h a b", a=TOP),
                                           tv4[:, :, 0, :].unsqueeze(3).broadcast_to((P, PH, TOP, TOP)),
                                           tv4[:, :, 1, :].unsqueeze(2).broadcast_to((P, PH, TOP, TOP)), ALU.add))
                    link(top16(cs, pos.rearrange("p (a b) -> p a b", a=PH), cand, PH))
                    dve.tensor_tensor(gs[:, bass.ds(m * PH, PH), :], cs, cs[:, :, 0:1].broadcast_to((P, PH, TOP)),
                                      ALU.subtract)
                    dve.tensor_copy(tif.rearrange("p h s k -> p (h s k)"), ti.rearrange("p a b -> p (a b)"))
                    dve.tensor_scalar(pos12[:, 0, :], pos, 4, None, ALU.logical_shift_right)
                    link(dve.tensor_scalar(pos12[:, 1, :], pos, 15, None, ALU.bitwise_and))
                    link(dve.tensor_copy(posf.rearrange("p a b -> p (a b)"), pos12.rearrange("p a b -> p (a b)")))
                    for s in range(2):
                        link(dve.tensor_tensor(eq, posf[:, s, :].unsqueeze(2).broadcast_to((P, P, TOP)),
                                               iota[:, 0:TOP].unsqueeze(1).broadcast_to((P, P, TOP)), ALU.is_equal))
                        eq4 = eq.rearrange("p (h k) j -> p h k j", h=PH)
                        link(dve.tensor_tensor(eq4, eq4, tif[:, :, s, :].unsqueeze(2).broadcast_to((P, PH, TOP, TOP)),
                                               ALU.mult))
                        link(dve.tensor_reduce(eg[:, bass.ds(m, 1), s, :], eq, AXX, ALU.add))

                dve.wait_ge(act_free, A0[f"U{layer}"])
                loop(3, 1 + 3 + 1 + 1 + 3 + 1 + 2 + 6, route)
                dve.wait_ge(dstep, count["n"])
                dve.engine_nop().then_inc(exp_in, 1)
                dve.wait_ge(exp_out, layer + 1)
                link(dve.tensor_reduce(gsum, gs, AXX, ALU.add))
                link(dve.reciprocal(grec, gsum))
                for m in range(3):
                    last = dve.tensor_tensor(eg[:, m, 2, :].rearrange("p (h k) -> p h k", h=PH),
                                             gs[:, m * PH:(m + 1) * PH, :],
                                             grec[:, m * PH:(m + 1) * PH].unsqueeze(2).broadcast_to((P, PH, TOP)), ALU.mult)
                last.then_inc(slot_ready, 1)
                for m in range(3):
                    b = full(f"e{layer}", m)
                    dve.tensor_copy(slots[:, :, m * P:(m + 1) * P],
                                    ps[:, b, 0:3 * P].rearrange("p (a b) -> p a b", a=3)).then_inc(dve_free, 1)
                dve.wait_ge(dve_free, D0[f"e{layer}"] + 3)
                dve.tensor_copy(halves[:], slots[:, 0:2, :])
                for c in range(3):
                    link(dve.tensor_copy(parts[:, c, :], slots[:, 2, :]))
                    if c < 2:
                        link(dve.tensor_tensor(slots[:, 2, :], slots[:, 2, :], parts[:, c, :], ALU.subtract))

                def one_hot_group(q, j, it):
                    s = j % RH
                    tok = j * GT if it is None else it * (HALF * GT) + j * GT
                    link(dve.tensor_tensor(here2[:, s], iota16[:, q * EQ:(q + 1) * EQ].unsqueeze(1).broadcast_to((P, GT, EQ)),
                                           halves[:, 1, bass.ds(tok, GT)].unsqueeze(2).broadcast_to((P, GT, EQ)),
                                           ALU.is_equal))
                    dve.tensor_tensor(hot1[:, s], iota16[:].unsqueeze(1).broadcast_to((P, GT, NK)),
                                      halves[:, 0, bass.ds(tok, GT)].unsqueeze(2).broadcast_to((P, GT, NK)),
                                      ALU.is_equal)
                    dve.tensor_tensor(hot2[:, s], here2[:, s].unsqueeze(1).broadcast_to((P, 3, GT, EQ)),
                                      parts[:, :, bass.ds(tok, GT)].unsqueeze(3).broadcast_to((P, 3, GT, EQ)),
                                      ALU.mult).then_inc(hot_ready, 1)

                def gate_groups(q, first, n, it):
                    nth = layer * NQ + q
                    for j in range(first, first + n):
                        dve.wait_ge(gate_full, it * HALF + (nth * NGG + j + 1))
                        dst = C[:, q % 2, :, bass.ds(it * (HALF * GT) + j * GT, GT)]
                        src = ps[:, 6 + j % 2, 0:GT * EQ].rearrange("p (t e) -> p e t", t=GT)
                        dve.tensor_tensor(dst, dst, src, ALU.mult).then_inc(gate_free, 1)
                        one_hot_group(q, j + LEAD, it)

                def before_gates(q):
                    dve.wait_ge(act_free, A0[f"U{layer}"] + (q + 1) * EQ)
                    for j in range(LEAD):
                        one_hot_group(q, j, None)

                def quarter(q, gq):
                    k0 = None if q is None else D0[f"V{layer}"] + q * DC

                    def body(it):
                        for dc in range(4):
                            if gq is not None:
                                first, last = due(dc, 4), due(dc + 1, 4)
                                gate_groups(gq, first, last - first, it)
                            if q is not None:
                                dve.wait_ge(dve_full, it * 4 + (k0 + dc + 1))
                                dst = xT[:, bass.ds(it * 4 + dc, 1), :]
                                dve.tensor_tensor(dst, dst, ps[:, 4 + dc % 2:5 + dc % 2, 0:T],
                                                  ALU.add).then_inc(dve_free, 1)

                    if gq is not None:
                        before_gates(gq)
                    loop(2, HALF if gq is not None else 0, body)

                quarter(None, 0)
                for q in range(NQ):
                    quarter(q, q + 1 if q + 1 < NQ else None)
                dve.wait_ge(dve_free, D0[f"V{layer}"] + NQ * DC)
                dve.engine_nop().then_inc(x_ready, 1)

            peer(0)

            norm("nb", 4, 2)
            dve.wait_ge(act_free, A0["qb"])
            scaled(3)
            for b_ in range(NB):
                dve.wait_ge(k_landed[b_ % 2], 16 * NG * (b_ // 2 + 1))
                for g in range(NG):
                    n = CK[g]
                    for pr in range(2):
                        b = full("qk", (b_ * NG + g) * 2 + pr)
                        if CS[g] == 1:
                            keys = Kc[0:n, b_ % 2, 0:256].unsqueeze(1).broadcast_to((n, 2, 256))
                        else:
                            at = COFF[g] + 2 * pr * 256
                            keys = Kc[0:n, b_ % 2, at:at + 512].rearrange("p (a b) -> p a b", a=2)
                        dve.tensor_tensor(prod[0:n, 8 * pr:8 * pr + 8, :].rearrange("p (a h) e -> p a (h e)", a=2),
                                          keys, ps[0:n, b, :].rearrange("p (a b) -> p a b", a=2),
                                          ALU.mult).then_inc(dve_free, 1)
                    dve.wait_ge(dve_free, D0["qk"] + (b_ * NG + g) * 2 + 2)
                    out = Sk[0:n, g, :].rearrange("p (h t) -> p t h", h=HPG)[:, NS * b_:NS * b_ + NS, :]
                    last = dve.tensor_reduce(out, prod[0:n].rearrange("p (t h) e -> p t h e", h=HPG), AXX, ALU.add)
                    if g < NG - 1:
                        link(last)
                last.then_inc(k_used, 1)
                dve.wait_ge(k_used, b_ + 1)
            b = full("sc", 0)
            dve.tensor_tensor(Ss[:, 0:320], sbias[:, 0:320], ps[:, b, 0:320], ALU.add).then_inc(dve_free, 1)
            for par in range(2):
                b = full("sc", 1 + par)
                for h in (par, par + 2):
                    rows = slice(32 * h, 32 * h + 32)
                    last = dve.tensor_tensor(Ss[rows, 320:SCOLS], sbias[rows, 320:SCOLS], ps[rows, b, 0:96], ALU.add)
                last.then_inc(dve_free, 1)
            dve.wait_ge(dve_free, D0["ps"])
            link(dve.reduce_max(stat[:, 9:10], Ss, AXX))
            dve.tensor_scalar(stat[:, 9:10], stat[:, 9:10], -1.0, None, ALU.mult).then_inc(sm_in, 1)
            dve.wait_ge(sm_exp, 1)
            link(dve.reciprocal(stat[:, 10:11], stat[:, 10:11]))
            dve.tensor_scalar(Ss, Ss, stat[:, 10:11], None, ALU.mult).then_inc(sm_out, 1)
            dve.wait_ge(dist_loaded, 16)
            for u in range(8):
                h, m = u // 2, u % 2
                n = P * (m + 1)
                if u:
                    dve.wait_ge(act_free, A0["pp"] + sum(3 if w % 2 else 2 for w in range(u)))
                for g in range(NG):
                    b = full("ps", 3 * u + g)
                    dve.scalar_tensor_tensor(out=Pp[:, g, 0:n], in0=dist[:, g, m, 0:n], scalar=SLOPES[g * HPG + h],
                                             in1=ps[:, b, 0:n], op0=ALU.mult, op1=ALU.add).then_inc(dve_free, 1)
                dve.wait_ge(dve_free, D0["ps"] + 3 * u + 3)
                link(dve.tensor_reduce(stat[:, 11:12], Pp[:, :, 0:n], mybir.AxisListType.XY, ALU.max))
                dve.tensor_scalar(stat[:, 11:12], stat[:, 11:12], -1.0, None, ALU.mult).then_inc(pp_in, 1)
                dve.wait_ge(pp_exp, u + 1)
                link(dve.reciprocal(stat[:, 12:13], stat[:, 12:13]))
                dve.tensor_scalar(Pp[:, :, 0:n], Pp[:, :, 0:n], stat[:, 12:13], None, ALU.mult).then_inc(pp_out, 1)
            add_chunks("ob")
            peer(1)
            norm("nf", 6, 5)


def _lhs_blocks(w):
    m = w.shape[1] // 256
    return w.reshape(8, 128, m, 2, 128).transpose(2, 1, 3, 0, 4).reshape(m, 128, 2048)


def _constants():
    r = np.arange(128)
    out = {"ident": np.eye(128), "iota": np.tile(r, (128, 1)), "maskp": r[:, None] <= r[None, :]}
    s = np.arange(32)
    out["masks"] = (s[:, None] // 4 == s[None, :] // 4) & (s[:, None] <= s[None, :])
    dist = np.zeros((128, 3, 2, 256))
    for g, (w, d) in enumerate(zip(WINDOWS, DILS)):
        i, j = np.arange(256)[:, None], np.arange(256)[None, :]
        ok = (j <= i) & ((i - j) % d == 0) & (i - j <= w)
        dist[:, g] = np.where(ok, -(i - j), -1e30).reshape(2, 128, 256).transpose(1, 0, 2)
    out["dist"] = dist
    bias = np.zeros((4, 32, SCOLS))
    for h in range(4):
        for t in range(32):
            b, s_ = divmod(t, 4)
            row = bias[h, t]
            k = np.arange(128)
            row[0:128] = np.where(k >= s_, -SLOPES[h] * (128 + s_ - k), -1e30)
            row[128:256] = -SLOPES[4 + h] * 4 * (128 - k)
            k = np.arange(64)
            row[256:320] = -SLOPES[8 + h] * 16 * (64 - k)
            n = np.arange(32)
            row[320:352] = np.where((n // 4 == b) & (n <= t), -SLOPES[h] * (t - n), -1e30)
            row[352:384] = np.where(n == t, 0.0, -1e30)
            row[384:416] = np.where(n == t, 0.0, -1e30)
    out["sbias"] = bias.reshape(128, SCOLS)
    return {k: np.ascontiguousarray(v, dtype=np.float32) for k, v in out.items()}


def _layout(a):
    x = np.concatenate([a["x_prompt"].reshape(256, 1024), a["x_sample"].reshape(32, 1024)])
    i = dict(_constants())
    i["xT"] = x.T.reshape(8, 128, 288).transpose(1, 0, 2)
    g = np.stack([a["a_norm"][0], a["ffn_norm"][0], a["kv_norm"], a["b_norm"][0], a["ffn_norm"][1], a["final_norm"]])
    i["gains"] = g.reshape(6, 8, 128).transpose(2, 0, 1)
    i["vgain"] = a["a_v_norm"][0]
    w_in = a["a_w_in"][0]
    i["w_in_u"] = _lhs_blocks(w_in[:, :2048])
    i["w_in_v"] = w_in[:, 2048:].reshape(2, 4, 128, 4, 512).transpose(3, 0, 2, 1, 4).reshape(8, 128, 2048)
    ws = a["a_w_s"][0]
    i["wsp"] = ws.transpose(2, 0, 1)
    i["wss"] = np.tile(ws[:, :4, :4].transpose(2, 0, 1), (8, 1, 8))
    i["bsp"] = a["a_b_s"][0]
    i["bss"] = np.tile(a["a_b_s"][0][:, :4], (1, 8))
    i["w_out"] = a["a_w_out"][0].reshape(16, 128, 8, 128).transpose(2, 1, 0, 3).reshape(8, 128, 2048)
    i["w_k"] = _lhs_blocks(a["w_kv"][:, :768])
    i["w_v"] = a["w_kv"][:, 768:].reshape(8, 128, 3, 256).transpose(2, 1, 0, 3).reshape(3, 128, 2048)
    i["w_q"] = _lhs_blocks(a["b_w_q"][0])
    i["w_o"] = a["b_w_o"][0].reshape(6, 128, 8, 128).transpose(1, 2, 0, 3).reshape(128, 3, 2048).transpose(1, 0, 2)
    i["skT"] = a["peer_sub_keys"].transpose(3, 0, 1, 2)
    for n in range(2):
        i[f"peer_q{n}"] = _lhs_blocks(a["peer_w_q"][n])
        i[f"U{n}"] = a["peer_u"][n].reshape(128, 64, 2, 8, 128).transpose(1, 4, 2, 3, 0).reshape(64, 128, 2048)
        i[f"V{n}"] = a["peer_v"][n].reshape(128, 4, 2, 16, 8, 128).transpose(1, 4, 2, 0, 3, 5).reshape(64, 128, 2048)
    for n, w in enumerate((128, 512, 2048)):
        c = a[f"cache_kv_w{w}"]
        i[f"cache{n}"] = c.reshape(8, c.shape[1], 2, 256)
    return i


_OUTS = {"yT": (128, 8, 288), "a_v_prompt": (128, 2048), "a_v_sample": (32, 2048), "kT": (128, 6, 288),
         "v_prompt": (128, 2, 768), "v_sample": (32, 768)}


def kernel(**inputs):
    import concourse.bacc as _bacc
    from concourse.bass_utils import run_bass_kernel_spmd as _run

    laid = {k: np.ascontiguousarray(v) for k, v in _layout({k: np.asarray(v) for k, v in inputs.items()}).items()}
    nc = _bacc.Bacc("TRN2", target_bir_lowering=False, num_devices=1)
    ins = {k: nc.dram_tensor(f"in_{k}", v.shape, mybir.dt.from_np(v.dtype), kind="ExternalInput").ap()
           for k, v in laid.items()}
    outs = {k: nc.dram_tensor(f"out_{k}", s, F32, kind="ExternalOutput").ap() for k, s in _OUTS.items()}
    build(nc, ins, outs)
    r = _run(nc, [{f"in_{k}": v for k, v in laid.items()}], core_ids=[0]).results[0]
    y = r["out_yT"].transpose(2, 1, 0).reshape(288, 1024)
    k = r["out_kT"].transpose(2, 1, 0).reshape(288, 3, 4, 64)
    v = np.concatenate([r["out_v_prompt"].transpose(1, 0, 2).reshape(256, 768), r["out_v_sample"]]).reshape(288, 3, 4, 64)
    kv = np.stack([k, v], axis=1)
    prompt, sample = kv[None, :256], kv[256:].reshape(8, 4, 2, 3, 4, 64)
    return (y[None, :256], y[256:].reshape(8, 4, 1024),
            r["out_a_v_prompt"][None, None], r["out_a_v_sample"].reshape(1, 8, 4, 2048),
            prompt[:, 128:, :, 0], prompt[:, :, :, 1], prompt[:, :, :, 2],
            sample[:, :, :, 0], sample[:, :, :, 1], sample[:, :, :, 2])
```

```python
from contextlib import ExitStack

import numpy as np

import concourse.bass as bass
from concourse import mybir

F32 = mybir.dt.float32
BF16 = mybir.dt.bfloat16
F32R = mybir.dt.float32r
U32 = mybir.dt.uint32
ACT = mybir.ActivationFunctionType
ALU = mybir.AluOpType
AXX = mybir.AxisListType.X

P = 128
D = 1024
DC = D // P
NPROMPT, NB, NS = 256, 8, 4
NSAMP = NB * NS
T = NPROMPT + NSAMP
TILES = [(0, 128), (128, 128), (256, 32)]
EPS = 1e-6
DAV = 2 * D
FC = DAV // P
AG = 8
HP = 16
PH = 8
TOP = 16
NK = 128
NQ = 4
EQ = NK // NQ
GT = 8
NGG = T // GT
ALONE = 18
DOWN_PART, UP_PART = 12, 6
LEAD = 2
RH = 3
CREDIT = 3
NG, HPG, HD = 3, 4, 64
WINDOWS = (128, 512, 2048)
DILS = (1, 4, 16)
NHB = NG * HPG
AW = NHB * HD
AC = AW // P
PAST = 1024
SLOPES = [float(np.float32(2.0 ** (-8.0 * (i + 1) / NHB))) for i in range(NHB)]
CK = [128, 128, 64]
CS = [1, 4, 4]
COFF = [0, 256, 1280]
KV = 2304
SCOLS = sum(CK) + NG * NSAMP
BLK = 2048
R = 4
HBLK = BLK // 2
HI_SLOTS, LO_SLOTS = 4, 2
HI_LEAD = 3
SPLIT = 7 * EQ
CCHUNKS = [(0, 2), (2, 8), (8, 16), (16, 32)]
BIG = -3.0e38

TO_ACT = [("u", FC), ("v", 12), ("q0", HP), ("s0", 12), ("U0", NK),
          ("k", AC), ("vn", 9), ("qb", AC), ("qn", 2), ("sp", 2), ("so", 1), ("pp", 20),
          ("q1", HP), ("s1", 12), ("U1", NK)]
TO_DVE = [("na", 1), ("gate", FC), ("wo", DC), ("n0", 1), ("e0", 3), ("V0", NQ * DC),
          ("nb", 1), ("qk", 48), ("sc", 3), ("ps", 24), ("ob", DC), ("n1", 1), ("e1", 3),
          ("V1", NQ * DC), ("nf", 1)]


def due(done, of, groups):
    return done * groups // of


def starts(stages):
    at, out = 0, {}
    for name, n in stages:
        out[name] = at
        at += n
    return out


def build(nc, i, o):
    A0, D0 = starts(TO_ACT), starts(TO_DVE)
    with ExitStack() as ctx:
        def sem(name):
            return ctx.enter_context(nc.semaphore(name))

        cursor = {"at": (nc.sbuf_base + 31) // 32 * 32}

        def at_address(name, at, shape, dt=F32):
            return nc.alloc_sbuf_tensor_at(name, shape, dt, offset=at)

        def place(name, shape, dt=F32):
            at = cursor["at"]
            size = int(np.prod(shape[1:])) * (2 if dt == BF16 else 4)
            cursor["at"] = at + (size + 31) // 32 * 32
            return at_address(name, at, shape, dt), at

        xT, _ = place("xT", [P, DC, T])
        ring, _ = place("ring", [P, R, BLK])
        wide, wide_at = place("wide", [P, 16 * T])
        h_hi = at_address("h_hi", wide_at, [P, DC, T], F32R)
        h_lo = at_address("h_lo", wide_at + 4 * DC * T, [P, DC, T], F32R)
        mid, mid_at = place("mid", [P, 3 * DAV])
        w_hi = at_address("w_hi", mid_at, [P, HI_SLOTS, HBLK], F32R)
        w_lo = at_address("w_lo", mid_at + 4 * HI_SLOTS * HBLK, [P, LO_SLOTS, HBLK], F32R)
        big, big_at = place("big", [P, 2 * EQ * T])
        C_lo = at_address("C_lo", big_at, [P, 2, EQ, T], F32R)
        stat, _ = place("stat", [P, 16])
        halves, _ = place("halves", [P, 2, 3 * P], BF16)
        parts, _ = place("parts", [P, 3, 3 * P], BF16)
        iota16, _ = place("iota16", [P, NK], BF16)
        iota_top, _ = place("iota_top", [P, TOP])
        ident, _ = place("ident", [P, P])
        ones, _ = place("ones", [P, P])
        gains, _ = place("gains", [P, 6, DC])
        hots, hots_at = place("hots", [P, 2816])
        work = at_address("work", hots_at, [P, 5632])
        C_hi, shared_at = place("C_hi", [P, EQ, T], F32R)
        cursor["at"] = hots_at + 4 * 5632
        hT, _ = place("hT", [P, DC, T])
        rs, _ = place("rs", [P, 3, T])
        slots, _ = place("slots", [P, 3, 3 * P])
        skT, _ = place("skT", [P, 2, 2, NK])
        sbias, _ = place("sbias", [P, SCOLS])
        iota, _ = place("iota", [P, P])
        assert cursor["at"] <= shared_at + 4 * EQ * T
        ps = ctx.enter_context(nc.psum_tensor("ps", [P, 8, 512], F32))

        def view(t, at, *shape, parts=P):
            n = int(np.prod(shape))
            v = t[0:parts, at:at + n]
            if len(shape) == 1:
                return v
            names = "abcd"[:len(shape)]
            return v.rearrange(f"p ({' '.join(names)}) -> p {' '.join(names)}",
                               **{c: s for c, s in zip(names, shape)})

        uT = view(wide, 0, FC, T)
        v = view(mid, 0, 3, DAV)
        vgain = view(big, 0, DAV)
        bsp = view(big, DAV, AG, P)
        bss = view(big, DAV + AG * P, AG, NSAMP)
        wsp = view(big, 3328, AG, P)
        wss = view(big, 4352, AG, NSAMP)
        maskp = view(big, 4608, P)
        masks = view(big, 4736, NSAMP)
        qT = view(wide, 0, HP, T)
        S3 = view(mid, 0, 3, HP * NK)
        S = view(big, EQ * T, HP, NK)
        cand = view(big, EQ * T + 2048, PH, TOP * TOP)
        eq = view(big, EQ * T + 4096, PH * TOP, TOP)
        tv = view(work, 0, HP, TOP)
        ti = work[:, 256:512].bitcast(U32).rearrange("p (a b) -> p a b", a=HP)
        tif = view(work, 512, PH, 2, TOP)
        cs = view(work, 768, PH, TOP)
        pos = work[:, 896:1024].bitcast(U32)
        pos12 = work[:, 1024:1280].bitcast(U32).rearrange("p (a b) -> p a b", a=2)
        posf = view(work, 1280, 2, PH * TOP)
        gs = view(work, 1536, 3 * PH, TOP)
        gsum = view(work, 1920, 3 * PH)
        grec = view(work, 1944, 3 * PH)
        eg = view(work, 1968, 3, 3, P)
        hot1 = hots[:, 0:1536].bitcast(BF16).rearrange("p (r t e) -> p r t e", r=RH, t=GT)
        hot2 = hots[:, 1536:2688].bitcast(BF16).rearrange("p (r c t e) -> p r c t e", r=RH, c=3, t=GT)
        here2 = hots[:, 2688:2816].bitcast(BF16).rearrange("p (t e) -> p t e", t=GT)
        C = view(big, 0, 2, EQ, T)
        aq = view(wide, 0, AC, T)
        ak = view(wide, AC * T, AC, T)
        Sk = view(wide, 2 * AC * T, NG, P)
        Ss = view(wide, 2 * AC * T + 384, SCOLS)
        av = view(mid, 0, 3, AW)
        dist = view(mid, 2304, NG, 2, 256)
        Pp = view(mid, 3840, NG, 256)
        PpT = view(mid, 4608, 6, P)
        PsT = view(mid, 5376, 6, P)
        Vc = view(big, 0, NB, KV)
        Kc = view(work, 0, 2, KV)
        prod = view(work, 2 * KV, 16, HD)
        qn = slots[0:NSAMP].rearrange("p a b -> p (a b)")[:, 0:AW]

        landed = [sem(f"landed{r}") for r in range(R)]
        blocks_begun = sem("blocks_begun")
        x_loaded, consts_loaded, mix_loaded = sem("x_loaded"), sem("consts_loaded"), sem("mix_loaded")
        act_full, act_free = sem("act_full"), sem("act_free")
        dve_full, dve_free = sem("dve_full"), sem("dve_free")
        ones_set = sem("ones_set")
        x_ready = sem("x_ready")
        squares = sem("squares")
        ms_ready, root_ready = sem("ms_ready"), sem("root_ready")
        h_ready = sem("h_ready")
        hi_made, lo_made = sem("hi_made"), sem("lo_made")
        halves_begun = sem("halves_begun")
        h_hi_made, h_lo_made = sem("h_hi_made"), sem("h_lo_made")
        C_hi_made, C_lo_made = sem("C_hi_made"), sem("C_lo_made")
        rows_cleared = sem("rows_cleared")
        sub_keys_loaded, sbias_loaded = sem("sub_keys_loaded"), sem("sbias_loaded")
        v_square, v_ready, ws_ready, ug_ready = sem("v_square"), sem("v_ready"), sem("ws_ready"), sem("ug_ready")
        exp_in, exp_out = sem("exp_in"), sem("exp_out")
        slot_ready = sem("slot_ready")
        hot_ready = sem("hot_ready")
        gate_full, gate_free = sem("gate_full"), sem("gate_free")
        dstep = sem("dstep")
        vc_loaded, dist_loaded = sem("vc_loaded"), sem("dist_loaded")
        k_landed = [sem("k_landed0"), sem("k_landed1")]
        k_used = sem("k_used")
        sm_in, sm_exp, sm_out = sem("sm_in"), sem("sm_exp"), sem("sm_out")
        pp_in, pp_exp, pp_out = sem("pp_in"), sem("pp_exp"), sem("pp_out")
        moved = sem("moved")
        av_saved, kv_saved, out_done = sem("av_saved"), sem("kv_saved"), sem("out_done")

        block = ctx.enter_context(nc.Block())

        @block.sync
        def _(sp):
            sp.dma_start(xT[:], i["xT"]).then_inc(x_loaded, 16)
            n = 0
            lo_base = split_end = 0
            for name in ("w_in_u", "w_in_v", "w_out", "peer_q0", "U0", "V0", "w_k", "w_v", "w_q",
                         "w_o", "peer_q1", "U1", "V1"):
                if name.startswith("V"):
                    continue
                src = i[name]
                if name.startswith("U"):
                    vsrc = i["V" + name[1]]
                    per = 64 // NQ
                    order = [(src, 0), (src, per)]
                    for q in range(NQ):
                        order.append((vsrc, q * per))
                        if q + 2 < NQ:
                            order.append((src, (q + 2) * per))
                    for k, (s, b0) in enumerate(order):
                        peel = 1 if k == 1 else 0
                        if peel:
                            first_split = n
                            for r in range(R):
                                sp.wait_ge(blocks_begun, n + r - R + 2)
                                sp.dma_start(ring[:, r, :], s[b0 + r]).then_inc(landed[r], 16)
                        with sp.Fori(peel, per // R) as it:
                            for r in range(R):
                                if k == 0:
                                    sp.wait_ge(blocks_begun, it * R + (n + r - R + 2))
                                else:
                                    sp.wait_ge(lo_made, it * (2 * R) + (lo_base + 2 * (n - first_split + r - R + 1)))
                                sp.dma_start(ring[:, r, :], s[it * R + (b0 + r)]).then_inc(landed[r], 16)
                        n += per
                    lo_base += SPLIT
                    split_end = n
                    continue
                for b in range(src.shape[0]):
                    if n < split_end + R and split_end:
                        sp.wait_ge(lo_made, lo_base + 2 * (n - R + 1 - split_end))
                    elif n >= R:
                        sp.wait_ge(blocks_begun, n - R + 2)
                    sp.dma_start(ring[:, n % R, :], src[b]).then_inc(landed[n % R], 16)
                    n += 1

        @block.gpsimd
        def _(pool):
            pool.memset(ones[:], 1.0)
            pool.memset(S3[:, 2, :], 0.0).then_inc(ones_set, 1)
            for t, s in ((ident[:], "ident"), (iota[:], "iota"), (gains[:], "gains")):
                pool.dma_start(t, i[s]).then_inc(consts_loaded, 16)
            pool.dma_start(skT[:], i["skT"]).then_inc(sub_keys_loaded, 16)
            pool.dma_start(vgain, i["vgain"].partition_broadcast(P)).then_inc(mix_loaded, 16)
            pool.dma_start(bsp, i["bsp"].partition_broadcast(P)).then_inc(mix_loaded, 16)
            pool.dma_start(bss, i["bss"].partition_broadcast(P)).then_inc(mix_loaded, 16)
            pool.dma_start(wsp, i["wsp"]).then_inc(mix_loaded, 16)
            pool.dma_start(wss[0:NSAMP], i["wss"]).then_inc(mix_loaded, 16)
            pool.dma_start(maskp, i["maskp"]).then_inc(mix_loaded, 16)
            pool.dma_start(masks[0:NSAMP], i["masks"]).then_inc(mix_loaded, 16)
            pool.wait_ge(v_ready, 1)
            pool.dma_start(o["a_v_prompt"], v[:, 1, :]).then_inc(av_saved, 16)
            pool.dma_start(o["a_v_sample"], v[0:NSAMP, 2, :]).then_inc(av_saved, 16)

            def lower_parts(layer):
                pool.wait_ge(h_hi_made, layer + 1)
                pool.tensor_tensor(h_lo[:], hT[:], h_hi[:], ALU.subtract).then_inc(h_lo_made, 1)

                def ring_round(it):
                    for k in range(2 * R):
                        n = layer * SPLIT + k
                        pool.wait_ge(hi_made, n + 1 if it is None else it * (2 * R) + (n + 1))
                        if n >= LO_SLOTS or it is not None:
                            begun = n - LO_SLOTS + 2
                            pool.wait_ge(halves_begun, begun if it is None else it * (2 * R) + begun)
                        pool.tensor_tensor(w_lo[:, k % LO_SLOTS, :], ring[:, k // 2, (k % 2) * HBLK:(k % 2 + 1) * HBLK],
                                           w_hi[:, k % HI_SLOTS, :], ALU.subtract).then_inc(lo_made, 1)

                ring_round(None)
                with pool.Fori(1, SPLIT // (2 * R)) as it:
                    ring_round(it)

            lower_parts(0)
            pool.wait_ge(x_ready, 2)
            pool.dma_start(skT[:], i["skT"]).then_inc(sub_keys_loaded, 16)
            pool.dma_start(sbias[:], i["sbias"]).then_inc(sbias_loaded, 16)
            pool.dma_start(dist, i["dist"]).then_inc(dist_loaded, 16)
            cache = [i["cache0"], i["cache1"], i["cache2"]]

            def load_cache(dst, b, which, done):
                for g in range(NG):
                    n, s = CK[g], CS[g]
                    rows = cache[g][b].rearrange("(r s) k c -> r s k c", r=n)[:, 0:s, which, :]
                    d = dst[0:n, COFF[g]:COFF[g] + s * 256].rearrange("p (s c) -> p s c", s=s)
                    pool.dma_start(d, rows).then_inc(done, 16)

            for b in range(NB):
                if b >= 2:
                    pool.wait_ge(k_used, b - 1)
                load_cache(Kc[:, b % 2, :], b, 0, k_landed[b % 2])
                load_cache(Vc[:, b, :], b, 1, vc_loaded)
            pool.wait_ge(act_free, A0["qn"])
            pool.dma_start(o["kT"], ak).then_inc(kv_saved, 16)
            pool.dma_start(o["v_prompt"], av[:, 0:2, :]).then_inc(kv_saved, 16)
            pool.dma_start(o["v_sample"], av[0:NSAMP, 2, :]).then_inc(kv_saved, 16)
            pool.wait_ge(x_ready, 3)
            pool.memset(S3[:, 2, :], 0.0).then_inc(rows_cleared, 1)
            lower_parts(1)
            pool.wait_ge(h_ready, 6)
            pool.dma_start(o["yT"], hT[:]).then_inc(out_done, 16)
            pool.wait_ge(av_saved, 16 * 2)
            pool.wait_ge(kv_saved, 16 * 3)
            pool.wait_ge(out_done, 16)

        @block.tensor
        def _(pe):
            state = {"block": 0, "half": 0}

            def arrived(n, i4=None, rounds=0):
                want = 16 * (n // R + 1)
                pe.wait_ge(landed[n % R], want if i4 is None else i4 * (16 * rounds) + want)
                return n % R

            def act_bank(stage, k):
                if k < 4:
                    if A0[stage] > 0:
                        pe.wait_ge(act_free, A0[stage])
                else:
                    pe.wait_ge(act_free, A0[stage] + k - 3)
                return k % 4

            def dve_bank(stage, k):
                if k < 4:
                    if D0[stage] > 0:
                        pe.wait_ge(dve_free, D0[stage])
                else:
                    pe.wait_ge(dve_free, D0[stage] + k - 3)
                return 4 + k % 4

            def mean_square(stage, nth):
                pe.wait_ge(squares, nth)
                b = dve_bank(stage, 0)
                for c in range(DC):
                    last = pe.matmul(ps[:, b, 0:T], ones[:], hT[:, c, :], start=(c == 0), stop=(c == DC - 1))
                last.then_inc(dve_full, 1)

            def project(stage, nblocks):
                for bl in range(nblocks):
                    r = arrived(state["block"])
                    for j in range(2):
                        b = act_bank(stage, 2 * bl + j)
                        for c in range(DC):
                            at = (j * DC + c) * P
                            last = pe.matmul(ps[:, b, 0:T], ring[:, r, at:at + P], hT[:, c, :],
                                             start=(c == 0), stop=(c == DC - 1))
                            if c == 0 and j == 0:
                                last.then_inc(blocks_begun, 1)
                        last.then_inc(act_full, 1)
                    state["block"] += 1

            pe.wait_ge(ones_set, 1)
            mean_square("na", 1)
            pe.wait_ge(h_ready, 1)
            project("u", 8)
            for fg in range(4):
                n0 = state["block"]
                rr = [arrived(n0), arrived(n0 + 1)]
                for m, (t0, tn) in enumerate(TILES):
                    b = act_bank("v", 3 * fg + m)
                    for c in range(DC):
                        last = pe.matmul(ps[0:tn, b, :], hT[:, c, t0:t0 + tn],
                                         ring[:, rr[c // 4], (c % 4) * 512:(c % 4 + 1) * 512],
                                         start=(c == 0), stop=(c == DC - 1))
                        if (m, c) in ((0, 0), (2, 4)):
                            last.then_inc(blocks_begun, 1)
                    last.then_inc(act_full, 1)
                state["block"] += 2
            pe.wait_ge(v_ready, 1)
            pe.wait_ge(ws_ready, 1)
            for c in range(FC):
                b = dve_bank("gate", c)
                g = c * P // 256
                for m, (t0, tn) in enumerate(TILES):
                    w = wsp[:, g, :] if m < 2 else wss[0:NSAMP, g, :]
                    last = pe.matmul(ps[:, b, t0:t0 + tn], v[0:tn, m, c * P:(c + 1) * P], w, start=True, stop=True)
                last.then_inc(dve_full, 1)
            for c in range(DC):
                r = arrived(state["block"])
                b = dve_bank("wo", c)
                for f in range(FC):
                    if c == 0:
                        pe.wait_ge(ug_ready, f + 1)
                    last = pe.matmul(ps[:, b, 0:T], ring[:, r, f * P:(f + 1) * P], uT[:, f, :],
                                     start=(f == 0), stop=(f == FC - 1))
                    if f == 0:
                        last.then_inc(blocks_begun, 1)
                last.then_inc(dve_full, 1)
                state["block"] += 1

            def peer(layer):
                mean_square(f"n{layer}", 2 + 2 * layer)
                pe.wait_ge(h_ready, 2 + 3 * layer)
                project(f"q{layer}", 8)
                pe.wait_ge(act_free, A0[f"s{layer}"])
                pe.wait_ge(sub_keys_loaded, 16 * (layer + 1))
                for m, (t0, tn) in enumerate(TILES):
                    for g4 in range(4):
                        b = act_bank(f"s{layer}", 4 * m + g4)
                        for j in range(4):
                            hp = 4 * g4 + j
                            last = pe.matmul(ps[0:tn, b, j * NK:(j + 1) * NK], qT[:, hp, t0:t0 + tn],
                                             skT[:, layer, hp % 2, :], start=True, stop=True)
                        last.then_inc(act_full, 1)

                def slot_transposes():
                    for m in range(3):
                        pe.wait_ge(slot_ready, layer + 1)
                        b = dve_bank(f"e{layer}", m)
                        for a in range(3):
                            last = pe.transpose(ps[:, b, a * P:(a + 1) * P], eg[:, m, a, :], ident[:])
                        last.then_inc(dve_full, 1)

                def gate_groups(gates, done, of, it):
                    if gates is None:
                        return
                    q, first, n = gates
                    nth = layer * NQ + q
                    for j in range(due(done, of, n), due(done + 1, of, n)):
                        pe.wait_ge(hot_ready, it * n + (nth * (NGG + LEAD) + first + j + 1))
                        pe.wait_ge(gate_free, it * n + (nth * NGG + first + j - 1 + CREDIT))
                        for t in range(GT):
                            for c in range(3):
                                g = pe.matmul(ps[:, 6 + j % 2, t * EQ:(t + 1) * EQ], hot1[:, j % RH, t, :],
                                              hot2[:, j % RH, c, t, :], start=(c == 0), stop=(c == 2))
                        g.then_inc(gate_full, 1)

                def up_whole(q):
                    n0 = state["block"]
                    k0 = A0[f"U{layer}"] + q * EQ
                    with pe.Fori(0, 2) as it:
                        for bl in range(8):
                            r = arrived(n0 + bl, it, 2)
                            for j in range(2 * bl, 2 * bl + 2):
                                pe.wait_ge(act_free, it * 16 + (k0 + j - 3))
                                for c in range(DC):
                                    at = ((j % 2) * DC + c) * P
                                    last = pe.matmul(ps[:, j % 4, 0:T], ring[:, r, at:at + P], hT[:, c, :],
                                                     start=(c == 0), stop=(c == DC - 1))
                                    if c == 0 and j % 2 == 0:
                                        last.then_inc(blocks_begun, 1)
                                last.then_inc(act_full, 1)
                    state["block"] += EQ // 2

                def product(out, h, tile, hi, lo, start, stop):
                    at = slice(tile * P, (tile + 1) * P)
                    one = pe.matmul(out, w_hi[:, h % HI_SLOTS, at], hi, start=start, stop=False)
                    two = pe.matmul(out, w_hi[:, h % HI_SLOTS, at], lo, start=False, stop=False)
                    if tile == 0:
                        if h % 2 == 0:
                            one.then_inc(blocks_begun, 1)
                        two.then_inc(halves_begun, 1)
                    return pe.matmul(out, w_lo[:, h % LO_SLOTS, at], hi, start=False, stop=stop)

                def up(q, gates):
                    h0 = state["half"]
                    k0 = A0[f"U{layer}"] + q * EQ
                    with pe.Fori(0, 2) as it:
                        for h in range(16):
                            pe.wait_ge(lo_made, it * 16 + (h0 + h + 1))
                            pe.wait_ge(act_free, it * 16 + (k0 + h - 3))
                            for c in range(DC):
                                last = product(ps[:, h % 4, 0:T], h, c, h_hi[:, c, :], h_lo[:, c, :],
                                               c == 0, c == DC - 1)
                                if c == DC - 1:
                                    last.then_inc(act_full, 1)
                                gate_groups(gates, h * DC + c, 16 * DC, it)
                    state["half"] += EQ
                    state["block"] += EQ // 2

                def down(q, gates):
                    h0 = state["half"]
                    k0 = D0[f"V{layer}"] + q * DC
                    c0 = (layer * NQ + q) * len(CCHUNKS)
                    with pe.Fori(0, 2) as it:
                        for h in range(16):
                            dc = h // 4
                            if h % 4 == 0:
                                pe.wait_ge(dve_free, it * 4 + (k0 + dc - 1))
                            pe.wait_ge(lo_made, it * 16 + (h0 + h + 1))
                            for t in range(8):
                                e = (h % 4) * 8 + t
                                for k, (e0, _) in enumerate(CCHUNKS):
                                    if dc == 0 and e == e0:
                                        pe.wait_ge(C_lo_made, c0 + k + 1)
                                last = product(ps[:, 4 + dc % 2, 0:T], h, t, C_hi[:, e, :], C_lo[:, q % 2, e, :],
                                               e == 0, e == EQ - 1)
                                if e == EQ - 1:
                                    last.then_inc(dve_full, 1)
                                gate_groups(gates, h * 8 + t, 128, it)
                    state["half"] += EQ
                    state["block"] += EQ // 2

                up_whole(0)
                slot_transposes()
                pe.wait_ge(dve_free, D0[f"V{layer}"])
                pe.wait_ge(h_lo_made, layer + 1)
                up(1, (0, 0, ALONE))
                down(0, (1, 0, DOWN_PART))
                up(2, (1, 2 * DOWN_PART, UP_PART))
                down(1, (2, 0, DOWN_PART))
                up(3, (2, 2 * DOWN_PART, UP_PART))
                down(2, (3, 0, ALONE))
                down(3, None)

            peer(0)

            mean_square("nb", 3)
            pe.wait_ge(h_ready, 3)
            project("k", 3)
            for fg in range(3):
                r = arrived(state["block"])
                for m, (t0, tn) in enumerate(TILES):
                    b = act_bank("vn", 3 * fg + m)
                    for c in range(DC):
                        last = pe.matmul(ps[0:tn, b, 0:256], hT[:, c, t0:t0 + tn], ring[:, r, c * 256:(c + 1) * 256],
                                         start=(c == 0), stop=(c == DC - 1))
                        if m == 0 and c == 0:
                            last.then_inc(blocks_begun, 1)
                    last.then_inc(act_full, 1)
                state["block"] += 1
            pe.wait_ge(h_ready, 4)
            project("qb", 3)
            for k in range(2):
                b = act_bank("qn", k)
                for j in range(3):
                    last = pe.transpose(ps[0:NSAMP, b, j * P:(j + 1) * P], aq[:, 3 * k + j, NPROMPT:T], ident[:])
                last.then_inc(act_full, 1)
            pe.wait_ge(act_free, A0["sp"])
            for b_ in range(NB):
                for g in range(NG):
                    for pr in range(2):
                        b = dve_bank("qk", (b_ * NG + g) * 2 + pr)
                        for j in range(2):
                            tok = NS * b_ + 2 * pr + j
                            last = pe.matmul(ps[:, b, j * 256:(j + 1) * 256],
                                             ident[0:NSAMP, tok:tok + 1].broadcast_to((NSAMP, P)),
                                             qn[:, g * 256:(g + 1) * 256], start=True, stop=True)
                        last.then_inc(dve_full, 1)
            pe.wait_ge(k_used, NB)
            b = dve_bank("sc", 0)
            at = 0
            for g in range(NG):
                last = pe.transpose(ps[:, b, at:at + CK[g]], Sk[0:CK[g], g, :], ident[0:CK[g], 0:CK[g]])
                at += CK[g]
            last.then_inc(dve_full, 1)
            for par in range(2):
                b = dve_bank("sc", 1 + par)
                for h in (par, par + 2):
                    for g in range(NG):
                        row = par * HD
                        last = pe.matmul(ps[32 * h:32 * h + 32, b, g * NSAMP:(g + 1) * NSAMP],
                                         aq[row:row + HD, 2 * g + h // 2, NPROMPT:T],
                                         ak[row:row + HD, 2 * g + h // 2, NPROMPT:T], start=True, stop=True)
                last.then_inc(dve_full, 1)

            def prompt_scores(u):
                h, m = u // 2, u % 2
                row = (h % 2) * HD
                for g in range(NG):
                    b = dve_bank("ps", 3 * u + g)
                    pe.matmul(ps[:, b, 0:P * (m + 1)], aq[row:row + HD, 2 * g + h // 2, m * P:(m + 1) * P],
                              ak[row:row + HD, 2 * g + h // 2, 0:P * (m + 1)],
                              start=True, stop=True).then_inc(dve_full, 1)

            pe.wait_ge(sm_out, 1)
            b = act_bank("sp", 0)
            at = 0
            for g in range(NG):
                last = pe.transpose(ps[0:CK[g], b, g * P:(g + 1) * P], Ss[:, at:at + CK[g]], ident[:])
                at += CK[g]
            last.then_inc(act_full, 1)
            b = act_bank("sp", 1)
            for g in range(NG):
                last = pe.transpose(ps[0:NSAMP, b, g * P:(g + 1) * P], Ss[:, at:at + NSAMP], ident[:])
                at += NSAMP
            last.then_inc(act_full, 1)
            pe.wait_ge(vc_loaded, 16 * NG * NB)
            b = act_bank("so", 0)
            for g in range(NG):
                for pr in range(2):
                    dst = ps[:, b, (g * 2 + pr) * 64:(g * 2 + pr + 1) * 64]
                    dst3 = dst.rearrange("p (j t) -> p j t", j=2)
                    pe.matmul(dst, av[0:NSAMP, 2, g * 256 + pr * P:g * 256 + (pr + 1) * P],
                              PsT[0:NSAMP, 3 + g, pr * 64:(pr + 1) * 64], start=True, stop=False,
                              skip_group_check=True)
                    prob = PsT[0:CK[g], g, pr * 64:(pr + 1) * 64].rearrange("p (j t) -> p j t", j=2)
                    for b_ in range(NB):
                        for s in range(CS[g]):
                            w = NS // CS[g]
                            t0 = NS * b_ + s * w
                            at = COFF[g] + s * 256 + pr * P
                            last = pe.matmul(dst3[:, :, t0:t0 + w], Vc[0:CK[g], b_, at:at + P],
                                             prob[:, :, t0:t0 + w], start=False,
                                             stop=(b_ == NB - 1 and s == CS[g] - 1), skip_group_check=True)
            last.then_inc(act_full, 1)

            prompt_scores(0)
            kk = 0
            for u in range(8):
                h, m = u // 2, u % 2
                if u + 1 < 8:
                    prompt_scores(u + 1)
                pe.wait_ge(pp_out, u + 1)
                for half in range(m + 1):
                    b = act_bank("pp", kk)
                    kk += 1
                    for g in range(NG):
                        last = pe.transpose(ps[:, b, g * P:(g + 1) * P], Pp[:, g, half * P:(half + 1) * P], ident[:])
                    last.then_inc(act_full, 1)
                b = act_bank("pp", kk)
                pe.wait_ge(act_free, A0["pp"] + kk)
                kk += 1
                row = (h % 2) * HD
                for g in range(NG):
                    f0 = g * 256 + h * HD
                    for half in range(m + 1):
                        last = pe.matmul(ps[row:row + HD, b, g * P:(g + 1) * P], av[:, half, f0:f0 + HD],
                                         PpT[:, half * 3 + g, :], start=(half == 0), stop=(half == m))
                last.then_inc(act_full, 1)
            pe.wait_ge(act_free, A0["q1"])
            for c in range(DC):
                b = dve_bank("ob", c)
                for f in range(AC):
                    k = c * AC + f
                    if k % 16 == 0:
                        r = arrived(state["block"])
                    last = pe.matmul(ps[:, b, 0:T], ring[:, r, (k % 16) * P:(k % 16 + 1) * P], hT[:, f, :],
                                     start=(f == 0), stop=(f == AC - 1))
                    if k % 16 == 0:
                        last.then_inc(blocks_begun, 1)
                        state["block"] += 1
                last.then_inc(dve_full, 1)
            peer(1)
            mean_square("nf", 5)

        first_split_block = [8 + 8 + DC + 8 + EQ // 2]
        first_split_block.append(first_split_block[0] + SPLIT // 2 + 3 + 3 + 3 + 3 + 8 + EQ // 2)

        @block.scalar
        def _(act):
            def full(stage, k):
                act.wait_ge(act_full, A0[stage] + k + 1)
                return k % 4

            def norm_part(nth):
                act.wait_ge(x_ready, nth - 1) if nth > 1 else act.wait_ge(x_loaded, 16)
                act.activation(hT[:], xT[:], ACT.Square).then_inc(squares, 1)
                act.wait_ge(ms_ready, nth if nth == 1 else nth + 1)
                act.activation(rs[:, 1, :], rs[:, 0, :], ACT.Sqrt).then_inc(root_ready, 1)

            act.wait_ge(ones_set, 1)
            norm_part(1)
            for c in range(FC):
                b = full("u", c)
                act.activation(uT[:, c, :], ps[:, b, 0:T], ACT.Gelu_apprx_tanh).then_inc(act_free, 1)
            for fg in range(4):
                for m, (t0, tn) in enumerate(TILES):
                    b = full("v", 3 * fg + m)
                    act.activation(v[0:tn, m, fg * 512:(fg + 1) * 512], ps[0:tn, b, :],
                                   ACT.Gelu_apprx_tanh).then_inc(act_free, 1)
            act.wait_ge(act_free, A0["q0"])
            act.wait_ge(moved, 1)
            for m, (t0, tn) in enumerate(TILES):
                junk = work[0:tn, m * DAV:(m + 1) * DAV] if m < 2 else view(hT.rearrange("p a b -> p (a b)"), 0, DAV, parts=tn)
                last = act.activation(junk, v[0:tn, m, :], ACT.Square, accum_out=stat[0:tn, m:m + 1])
            last.then_inc(v_square, 1)
            act.wait_ge(ms_ready, 2)
            act.activation(stat[:, 6:9], stat[:, 3:6], ACT.Sqrt).then_inc(root_ready, 1)

            def peer(layer):
                norm_part(2 + 2 * layer)
                if layer == 1:
                    act.wait_ge(kv_saved, 16 * 3)
                for c in range(HP):
                    b = full(f"q{layer}", c)
                    act.activation(qT[:, c, :], ps[:, b, 0:T], ACT.Copy).then_inc(act_free, 1)

                block0 = first_split_block[layer]

                def upper_part(k, it=None):
                    n = layer * SPLIT + k
                    bl = block0 + k // 2
                    want = 16 * (bl // R + 1)
                    act.wait_ge(landed[bl % R], want if it is None else it * 32 + want)
                    if n >= HI_SLOTS or it is not None:
                        begun = n - HI_SLOTS + 2
                        act.wait_ge(halves_begun, begun if it is None else it * 16 + begun)
                    act.activation(w_hi[:, k % HI_SLOTS, :], ring[:, bl % R, (k % 2) * HBLK:(k % 2 + 1) * HBLK],
                                   ACT.Copy).then_inc(hi_made, 1)

                def quarter(nth, q=None):
                    k0 = A0[f"U{layer}"] + (0 if q is None else q * EQ)
                    with act.Fori(0, 2) as it:
                        for h in range(16):
                            upper_part(nth * EQ + h + HI_LEAD, it)
                            if q is not None:
                                act.wait_ge(act_full, it * 16 + (k0 + h + 1))
                                act.activation(C[:, q % 2, it * 16 + h, :], ps[:, h % 4, 0:T],
                                               ACT.Gelu_apprx_tanh).then_inc(act_free, 1)

                def upper_C(q):
                    act.wait_ge(gate_free, (layer * NQ + q + 1) * NGG + CREDIT)
                    if q:
                        act.wait_ge(dve_full, D0[f"V{layer}"] + q * DC)
                    for e0, e1 in CCHUNKS:
                        act.activation(C_hi[:, e0:e1, :], C[:, q % 2, e0:e1, :], ACT.Copy).then_inc(C_hi_made, 1)

                if layer == 0:
                    act.wait_ge(av_saved, 16 * 2)
                else:
                    act.wait_ge(rows_cleared, 1)
                for m, (t0, tn) in enumerate(TILES):
                    for g4 in range(4):
                        b = full(f"s{layer}", 4 * m + g4)
                        act.activation(S3[0:tn, m, g4 * 512:(g4 + 1) * 512], ps[0:tn, b, :], ACT.Copy).then_inc(act_free, 1)
                act.activation(h_hi[:], hT[:], ACT.Copy).then_inc(h_hi_made, 1)
                k0 = A0[f"U{layer}"]
                with act.Fori(0, EQ // 8) as it:
                    for j in range(8):
                        act.wait_ge(act_full, it * 8 + (k0 + j + 1))
                        act.activation(C[:, 0, it * 8 + j, :], ps[:, j % 4, 0:T],
                                       ACT.Gelu_apprx_tanh).then_inc(act_free, 1)
                act.wait_ge(exp_in, layer + 1)
                act.activation(gs, gs, ACT.Exp).then_inc(exp_out, 1)
                for k in range(HI_LEAD):
                    upper_part(k)
                quarter(0, 1)
                upper_C(0)
                quarter(1)
                quarter(2, 2)
                upper_C(1)
                quarter(3)
                quarter(4, 3)
                upper_C(2)
                quarter(5)
                upper_C(3)
                for k in range(6 * EQ + HI_LEAD, SPLIT):
                    upper_part(k)

            peer(0)

            norm_part(3)
            for c in range(AC):
                b = full("k", c)
                act.activation(ak[:, c, :], ps[:, b, 0:T], ACT.Copy).then_inc(act_free, 1)
            for fg in range(3):
                for m, (t0, tn) in enumerate(TILES):
                    b = full("vn", 3 * fg + m)
                    act.activation(av[0:tn, m, fg * 256:(fg + 1) * 256], ps[0:tn, b, 0:256],
                                   ACT.Copy).then_inc(act_free, 1)
            for c in range(AC):
                b = full("qb", c)
                act.activation(aq[:, c, :], ps[:, b, 0:T], ACT.Copy, scale=HD ** -0.5).then_inc(act_free, 1)
            for k in range(2):
                b = full("qn", k)
                act.activation(qn[:, k * 384:(k + 1) * 384], ps[0:NSAMP, b, 0:384], ACT.Copy).then_inc(act_free, 1)
            act.wait_ge(sm_in, 1)
            act.activation(Ss, Ss, ACT.Exp, bias=stat[:, 9:10], accum_out=stat[:, 10:11]).then_inc(sm_exp, 1)
            b = full("sp", 0)
            act.activation(PsT[:, 0:2, :].rearrange("p a b -> p (a b)"), ps[:, b, 0:256], ACT.Copy)
            act.activation(PsT[0:CK[2], 2, :], ps[0:CK[2], b, 256:384], ACT.Copy).then_inc(act_free, 1)
            b = full("sp", 1)
            act.activation(PsT[0:NSAMP, 3:6, :].rearrange("p a b -> p (a b)"), ps[0:NSAMP, b, 0:384],
                           ACT.Copy).then_inc(act_free, 1)
            b = full("so", 0)
            o3 = ps[:, b, 0:384].rearrange("p (c j t) -> p c j t", c=AC, j=2)
            act.activation(hT[0:HD, 0:AC, NPROMPT:T], o3[0:HD, :, 0, :], ACT.Copy)
            act.activation(hT[HD:P, 0:AC, NPROMPT:T], o3[HD:P, :, 1, :], ACT.Copy).then_inc(act_free, 1)
            kk = 0
            for u in range(8):
                h, m = u // 2, u % 2
                row = (h % 2) * HD
                act.wait_ge(pp_in, u + 1)
                act.activation(Pp[:, :, 0:P * (m + 1)], Pp[:, :, 0:P * (m + 1)], ACT.Exp,
                               bias=stat[:, 11:12], accum_out=stat[:, 12:13]).then_inc(pp_exp, 1)
                for half in range(m + 1):
                    b = full("pp", kk)
                    kk += 1
                    act.activation(PpT[:, 3 * half:3 * half + 3, :].rearrange("p a b -> p (a b)"),
                                   ps[:, b, 0:384], ACT.Copy).then_inc(act_free, 1)
                b = full("pp", kk)
                kk += 1
                dst = hT[row:row + HD, :, m * P:(m + 1) * P]
                for g in range(NG):
                    last = act.activation(dst[:, 2 * g + h // 2, :], ps[row:row + HD, b, g * P:(g + 1) * P], ACT.Copy)
                last.then_inc(act_free, 1)
            peer(1)
            norm_part(5)

        @block.vector
        def _(dve):
            count = {"n": 0, "it": None, "per": 0}

            def step(ins):
                count["n"] += 1
                ins.then_inc(dstep, 1)

            def last_step():
                it = count["it"]
                dve.wait_ge(dstep, count["n"] if it is None else it * count["per"] + count["n"])

            def link(ins):
                step(ins)
                last_step()

            def loop(n, per, body):
                n0 = count["n"]
                with dve.Fori(0, n) as it:
                    count["it"], count["per"] = it, per
                    body(it)
                assert count["n"] == n0 + per, (count["n"] - n0, per)
                count["it"], count["n"] = None, n0 + n * per

            def full(stage, k):
                dve.wait_ge(dve_full, D0[stage] + k + 1)
                return 4 + k % 4

            def newton(r, ms, tmp):
                link(dve.tensor_tensor(tmp, r, r, ALU.mult))
                link(dve.tensor_tensor(tmp, tmp, ms, ALU.mult))
                link(dve.tensor_scalar(tmp, tmp, -0.5, 1.5, ALU.mult, ALU.add))
                link(dve.tensor_tensor(r, r, tmp, ALU.mult))

            def norm(stage, nth_root, gain):
                b = full(stage, 0)
                dve.tensor_scalar(rs[:, 0, :], ps[:, b, 0:T], 1.0 / D, EPS, ALU.mult, ALU.add).then_inc(dve_free, 1)
                dve.wait_ge(dve_free, D0[stage] + 1)
                dve.engine_nop().then_inc(ms_ready, 1)
                dve.wait_ge(root_ready, nth_root)
                link(dve.reciprocal(rs[:, 2, :], rs[:, 1, :]))
                newton(rs[:, 2, :], rs[:, 0, :], rs[:, 1, :])
                scaled(gain)

            def scaled(gain):
                for c in range(DC):
                    last = dve.scalar_tensor_tensor(out=hT[:, c, :], in0=xT[:, c, :], scalar=gains[:, gain, c:c + 1],
                                                    in1=rs[:, 2, :], op0=ALU.mult, op1=ALU.mult)
                last.then_inc(h_ready, 1)

            def add_chunks(stage):
                for c in range(DC):
                    b = full(stage, c)
                    dve.tensor_tensor(xT[:, c, :], xT[:, c, :], ps[:, b, 0:T], ALU.add).then_inc(dve_free, 1)
                dve.wait_ge(dve_free, D0[stage] + DC)
                dve.engine_nop().then_inc(x_ready, 1)

            dve.memset(stat[:], 1.0).then_inc(moved, 1)
            dve.engine_nop().then_inc(gate_free, CREDIT)
            dve.wait_ge(consts_loaded, 16 * 3)
            dve.tensor_copy(iota_top[:], iota[:, 0:TOP])
            dve.tensor_copy(iota16[:], iota[:])
            dve.wait_ge(x_loaded, 16)
            norm("na", 1, 0)
            dve.wait_ge(mix_loaded, 16 * 7)
            dve.tensor_tensor(wsp, wsp, maskp.unsqueeze(1).broadcast_to((P, AG, P)), ALU.mult)
            dve.tensor_tensor(wss[0:NSAMP], wss[0:NSAMP],
                              masks[0:NSAMP].unsqueeze(1).broadcast_to((NSAMP, AG, NSAMP)), ALU.mult).then_inc(ws_ready, 1)
            dve.wait_ge(v_square, 1)
            dve.tensor_scalar(stat[:, 3:6], stat[:, 0:3], 1.0 / DAV, EPS, ALU.mult, ALU.add).then_inc(ms_ready, 1)
            dve.wait_ge(root_ready, 2)
            link(dve.reciprocal(stat[:, 9:12], stat[:, 6:9]))
            newton(stat[:, 9:12], stat[:, 3:6], stat[:, 12:15])
            for m, (t0, tn) in enumerate(TILES):
                last = dve.scalar_tensor_tensor(out=v[0:tn, m, :], in0=v[0:tn, m, :], scalar=stat[0:tn, 9 + m:10 + m],
                                                in1=vgain[0:tn], op0=ALU.mult, op1=ALU.mult)
            last.then_inc(v_ready, 1)
            dve.wait_ge(act_free, FC)
            for c in range(FC):
                b = full("gate", c)
                g = c * P // 256
                dve.tensor_tensor(ps[:, b, 0:NPROMPT].rearrange("p (m t) -> p m t", m=2),
                                  ps[:, b, 0:NPROMPT].rearrange("p (m t) -> p m t", m=2),
                                  bsp[:, g:g + 1, :].broadcast_to((P, 2, P)), ALU.add)
                link(dve.tensor_tensor(ps[:, b, NPROMPT:T], ps[:, b, NPROMPT:T], bss[:, g, :], ALU.add))
                dve.tensor_tensor(uT[:, c, :], uT[:, c, :], ps[:, b, 0:T], ALU.mult).then_inc(dve_free, 1)
                dve.wait_ge(dve_free, D0["gate"] + c + 1)
                dve.engine_nop().then_inc(ug_ready, 1)
            add_chunks("wo")

            def peer(layer):
                norm(f"n{layer}", 3 + 2 * layer, 1 if layer == 0 else 4)

                def take_wait():
                    dve.memset(stat[:, 15:16], 0.0)

                def top16(val, idx, src, n):
                    take_wait()
                    for a in range(n):
                        last = dve.max(val[:, a, 0:8], src[:, a, :])
                    link(last)
                    take_wait()
                    for a in range(n):
                        dve.max_index(idx[:, a, 0:8], val[:, a, 0:8], src[:, a, :])
                    for a in range(n):
                        last = dve.match_replace(src[:, a, :], val[:, a, 0:8], src[:, a, :], BIG)
                    link(last)
                    take_wait()
                    for a in range(n):
                        last = dve.max(val[:, a, 8:16], src[:, a, :])
                    link(last)
                    take_wait()
                    for a in range(n):
                        last = dve.max_index(idx[:, a, 8:16], val[:, a, 8:16], src[:, a, :])
                    return last

                def route(m):
                    link(dve.tensor_copy(S.rearrange("p a b -> p (a b)").unsqueeze(1), S3[:, bass.ds(m, 1), :]))
                    link(top16(tv, ti, S, HP))
                    tv4 = tv.rearrange("p (h s) k -> p h s k", s=2)
                    link(dve.tensor_tensor(cand.rearrange("p h (a b) -> p h a b", a=TOP),
                                           tv4[:, :, 0, :].unsqueeze(3).broadcast_to((P, PH, TOP, TOP)),
                                           tv4[:, :, 1, :].unsqueeze(2).broadcast_to((P, PH, TOP, TOP)), ALU.add))
                    link(top16(cs, pos.rearrange("p (a b) -> p a b", a=PH), cand, PH))
                    dve.tensor_tensor(gs[:, bass.ds(m * PH, PH), :], cs, cs[:, :, 0:1].broadcast_to((P, PH, TOP)),
                                      ALU.subtract)
                    dve.tensor_copy(tif.rearrange("p h s k -> p (h s k)"), ti.rearrange("p a b -> p (a b)"))
                    dve.tensor_scalar(pos12[:, 0, :], pos, 4, None, ALU.logical_shift_right)
                    link(dve.tensor_scalar(pos12[:, 1, :], pos, 15, None, ALU.bitwise_and))
                    link(dve.tensor_copy(posf.rearrange("p a b -> p (a b)"), pos12.rearrange("p a b -> p (a b)")))
                    for s in range(2):
                        link(dve.tensor_tensor(eq, posf[:, s, :].unsqueeze(2).broadcast_to((P, P, TOP)),
                                               iota_top[:].unsqueeze(1).broadcast_to((P, P, TOP)), ALU.is_equal))
                        eq4 = eq.rearrange("p (h k) j -> p h k j", h=PH)
                        link(dve.tensor_tensor(eq4, eq4, tif[:, :, s, :].unsqueeze(2).broadcast_to((P, PH, TOP, TOP)),
                                               ALU.mult))
                        link(dve.tensor_reduce(eg[:, bass.ds(m, 1), s, :], eq, AXX, ALU.add))

                dve.wait_ge(act_free, A0[f"U{layer}"])
                loop(3, 1 + 3 + 1 + 1 + 3 + 1 + 2 + 6, route)
                dve.wait_ge(dstep, count["n"])
                dve.engine_nop().then_inc(exp_in, 1)
                dve.wait_ge(exp_out, layer + 1)
                link(dve.tensor_reduce(gsum, gs, AXX, ALU.add))
                link(dve.reciprocal(grec, gsum))
                for m in range(3):
                    last = dve.tensor_tensor(eg[:, m, 2, :].rearrange("p (h k) -> p h k", h=PH),
                                             gs[:, m * PH:(m + 1) * PH, :],
                                             grec[:, m * PH:(m + 1) * PH].unsqueeze(2).broadcast_to((P, PH, TOP)), ALU.mult)
                last.then_inc(slot_ready, 1)
                for m in range(3):
                    b = full(f"e{layer}", m)
                    dve.tensor_copy(slots[:, :, m * P:(m + 1) * P],
                                    ps[:, b, 0:3 * P].rearrange("p (a b) -> p a b", a=3)).then_inc(dve_free, 1)
                dve.wait_ge(dve_free, D0[f"e{layer}"] + 3)
                dve.tensor_copy(halves[:], slots[:, 0:2, :])
                for c in range(3):
                    link(dve.tensor_copy(parts[:, c, :], slots[:, 2, :]))
                    if c < 2:
                        link(dve.tensor_tensor(slots[:, 2, :], slots[:, 2, :], parts[:, c, :], ALU.subtract))

                def one_hot_group(q, j, it, per=0):
                    s = j % RH
                    tok = j * GT if it is None else it * (per * GT) + j * GT
                    before = (layer * NQ + q) * (NGG + LEAD) + j
                    if before:
                        dve.wait_ge(hot_ready, before if it is None else it * per + before)
                    step(dve.tensor_tensor(here2, iota16[:, q * EQ:(q + 1) * EQ].unsqueeze(1).broadcast_to((P, GT, EQ)),
                                           halves[:, 1, bass.ds(tok, GT)].unsqueeze(2).broadcast_to((P, GT, EQ)),
                                           ALU.is_equal))
                    dve.tensor_tensor(hot1[:, s], iota16[:].unsqueeze(1).broadcast_to((P, GT, NK)),
                                      halves[:, 0, bass.ds(tok, GT)].unsqueeze(2).broadcast_to((P, GT, NK)),
                                      ALU.is_equal)
                    last_step()
                    dve.tensor_tensor(hot2[:, s], here2.unsqueeze(1).broadcast_to((P, 3, GT, EQ)),
                                      parts[:, :, bass.ds(tok, GT)].unsqueeze(3).broadcast_to((P, 3, GT, EQ)),
                                      ALU.mult).then_inc(hot_ready, 1)

                def gate_groups(gates, done, of, it):
                    if gates is None:
                        return
                    q, first, n = gates
                    nth = layer * NQ + q
                    for k in range(due(done, of, n), due(done + 1, of, n)):
                        j = first + k
                        dve.wait_ge(gate_full, it * n + (nth * NGG + j + 1))
                        dst = C[:, q % 2, :, bass.ds(it * (n * GT) + j * GT, GT)]
                        src = ps[:, 6 + j % 2, 0:GT * EQ].rearrange("p (t e) -> p e t", t=GT)
                        dve.tensor_tensor(dst, dst, src, ALU.mult).then_inc(gate_free, 1)
                        one_hot_group(q, j + LEAD, it, n)

                def quarter(q, gates):
                    k0 = None if q is None else D0[f"V{layer}"] + q * DC

                    def body(it):
                        for dc in range(4):
                            gate_groups(gates, dc, 4, it)
                            if q is not None:
                                dve.wait_ge(dve_full, it * 4 + (k0 + dc + 1))
                                dst = xT[:, bass.ds(it * 4 + dc, 1), :]
                                dve.tensor_tensor(dst, dst, ps[:, 4 + dc % 2:5 + dc % 2, 0:T],
                                                  ALU.add).then_inc(dve_free, 1)

                    if gates is not None and gates[1] == 0:
                        dve.wait_ge(act_free, A0[f"U{layer}"] + (gates[0] + 1) * EQ)
                        for j in range(LEAD):
                            one_hot_group(gates[0], j, None)
                    loop(2, gates[2] if gates is not None else 0, body)

                def lower_C(q):
                    dve.wait_ge(gate_free, (layer * NQ + q + 1) * NGG + CREDIT)
                    for k, (e0, e1) in enumerate(CCHUNKS):
                        dve.wait_ge(C_hi_made, (layer * NQ + q) * len(CCHUNKS) + k + 1)
                        dve.tensor_tensor(C_lo[:, q % 2, e0:e1, :], C[:, q % 2, e0:e1, :], C_hi[:, e0:e1, :],
                                          ALU.subtract).then_inc(C_lo_made, 1)

                quarter(None, (0, 0, ALONE))
                lower_C(0)
                quarter(0, (1, 0, DOWN_PART))
                quarter(None, (1, 2 * DOWN_PART, UP_PART))
                lower_C(1)
                quarter(1, (2, 0, DOWN_PART))
                quarter(None, (2, 2 * DOWN_PART, UP_PART))
                lower_C(2)
                quarter(2, (3, 0, ALONE))
                lower_C(3)
                quarter(3, None)
                dve.wait_ge(dve_free, D0[f"V{layer}"] + NQ * DC)
                dve.engine_nop().then_inc(x_ready, 1)

            peer(0)

            norm("nb", 4, 2)
            dve.wait_ge(act_free, A0["qb"])
            scaled(3)
            for b_ in range(NB):
                dve.wait_ge(k_landed[b_ % 2], 16 * NG * (b_ // 2 + 1))
                for g in range(NG):
                    n = CK[g]
                    for pr in range(2):
                        b = full("qk", (b_ * NG + g) * 2 + pr)
                        if CS[g] == 1:
                            keys = Kc[0:n, b_ % 2, 0:256].unsqueeze(1).broadcast_to((n, 2, 256))
                        else:
                            at = COFF[g] + 2 * pr * 256
                            keys = Kc[0:n, b_ % 2, at:at + 512].rearrange("p (a b) -> p a b", a=2)
                        dve.tensor_tensor(prod[0:n, 8 * pr:8 * pr + 8, :].rearrange("p (a h) e -> p a (h e)", a=2),
                                          keys, ps[0:n, b, :].rearrange("p (a b) -> p a b", a=2),
                                          ALU.mult).then_inc(dve_free, 1)
                    dve.wait_ge(dve_free, D0["qk"] + (b_ * NG + g) * 2 + 2)
                    out = Sk[0:n, g, :].rearrange("p (h t) -> p t h", h=HPG)[:, NS * b_:NS * b_ + NS, :]
                    last = dve.tensor_reduce(out, prod[0:n].rearrange("p (t h) e -> p t h e", h=HPG), AXX, ALU.add)
                    if g < NG - 1:
                        link(last)
                last.then_inc(k_used, 1)
                dve.wait_ge(k_used, b_ + 1)
            dve.wait_ge(sbias_loaded, 16)
            b = full("sc", 0)
            dve.tensor_tensor(Ss[:, 0:320], sbias[:, 0:320], ps[:, b, 0:320], ALU.add).then_inc(dve_free, 1)
            for par in range(2):
                b = full("sc", 1 + par)
                for h in (par, par + 2):
                    rows = slice(32 * h, 32 * h + 32)
                    last = dve.tensor_tensor(Ss[rows, 320:SCOLS], sbias[rows, 320:SCOLS], ps[rows, b, 0:96], ALU.add)
                last.then_inc(dve_free, 1)
            dve.wait_ge(dve_free, D0["ps"])
            link(dve.reduce_max(stat[:, 9:10], Ss, AXX))
            dve.tensor_scalar(stat[:, 9:10], stat[:, 9:10], -1.0, None, ALU.mult).then_inc(sm_in, 1)
            dve.wait_ge(sm_exp, 1)
            link(dve.reciprocal(stat[:, 10:11], stat[:, 10:11]))
            dve.tensor_scalar(Ss, Ss, stat[:, 10:11], None, ALU.mult).then_inc(sm_out, 1)
            dve.wait_ge(dist_loaded, 16)
            for u in range(8):
                h, m = u // 2, u % 2
                n = P * (m + 1)
                if u:
                    dve.wait_ge(act_free, A0["pp"] + sum(3 if w % 2 else 2 for w in range(u)))
                for g in range(NG):
                    b = full("ps", 3 * u + g)
                    dve.scalar_tensor_tensor(out=Pp[:, g, 0:n], in0=dist[:, g, m, 0:n], scalar=SLOPES[g * HPG + h],
                                             in1=ps[:, b, 0:n], op0=ALU.mult, op1=ALU.add).then_inc(dve_free, 1)
                dve.wait_ge(dve_free, D0["ps"] + 3 * u + 3)
                link(dve.tensor_reduce(stat[:, 11:12], Pp[:, :, 0:n], mybir.AxisListType.XY, ALU.max))
                dve.tensor_scalar(stat[:, 11:12], stat[:, 11:12], -1.0, None, ALU.mult).then_inc(pp_in, 1)
                dve.wait_ge(pp_exp, u + 1)
                link(dve.reciprocal(stat[:, 12:13], stat[:, 12:13]))
                dve.tensor_scalar(Pp[:, :, 0:n], Pp[:, :, 0:n], stat[:, 12:13], None, ALU.mult).then_inc(pp_out, 1)
            add_chunks("ob")
            peer(1)
            norm("nf", 6, 5)


def _lhs_blocks(w):
    m = w.shape[1] // 256
    return w.reshape(8, 128, m, 2, 128).transpose(2, 1, 3, 0, 4).reshape(m, 128, 2048)


def _constants():
    r = np.arange(128)
    out = {"ident": np.eye(128), "iota": np.tile(r, (128, 1)), "maskp": r[:, None] <= r[None, :]}
    s = np.arange(32)
    out["masks"] = (s[:, None] // 4 == s[None, :] // 4) & (s[:, None] <= s[None, :])
    dist = np.zeros((128, 3, 2, 256))
    for g, (w, d) in enumerate(zip(WINDOWS, DILS)):
        i, j = np.arange(256)[:, None], np.arange(256)[None, :]
        ok = (j <= i) & ((i - j) % d == 0) & (i - j <= w)
        dist[:, g] = np.where(ok, -(i - j), -1e30).reshape(2, 128, 256).transpose(1, 0, 2)
    out["dist"] = dist
    bias = np.zeros((4, 32, SCOLS))
    for h in range(4):
        for t in range(32):
            b, s_ = divmod(t, 4)
            row = bias[h, t]
            k = np.arange(128)
            row[0:128] = np.where(k >= s_, -SLOPES[h] * (128 + s_ - k), -1e30)
            row[128:256] = -SLOPES[4 + h] * 4 * (128 - k)
            k = np.arange(64)
            row[256:320] = -SLOPES[8 + h] * 16 * (64 - k)
            n = np.arange(32)
            row[320:352] = np.where((n // 4 == b) & (n <= t), -SLOPES[h] * (t - n), -1e30)
            row[352:384] = np.where(n == t, 0.0, -1e30)
            row[384:416] = np.where(n == t, 0.0, -1e30)
    out["sbias"] = bias.reshape(128, SCOLS)
    return {k: np.ascontiguousarray(v, dtype=np.float32) for k, v in out.items()}


def _layout(a):
    x = np.concatenate([a["x_prompt"].reshape(256, 1024), a["x_sample"].reshape(32, 1024)])
    i = dict(_constants())
    i["xT"] = x.T.reshape(8, 128, 288).transpose(1, 0, 2)
    g = np.stack([a["a_norm"][0], a["ffn_norm"][0], a["kv_norm"], a["b_norm"][0], a["ffn_norm"][1], a["final_norm"]])
    i["gains"] = g.reshape(6, 8, 128).transpose(2, 0, 1)
    i["vgain"] = a["a_v_norm"][0]
    w_in = a["a_w_in"][0]
    i["w_in_u"] = _lhs_blocks(w_in[:, :2048])
    i["w_in_v"] = w_in[:, 2048:].reshape(2, 4, 128, 4, 512).transpose(3, 0, 2, 1, 4).reshape(8, 128, 2048)
    ws = a["a_w_s"][0]
    i["wsp"] = ws.transpose(2, 0, 1)
    i["wss"] = np.tile(ws[:, :4, :4].transpose(2, 0, 1), (8, 1, 8))
    i["bsp"] = a["a_b_s"][0]
    i["bss"] = np.tile(a["a_b_s"][0][:, :4], (1, 8))
    i["w_out"] = a["a_w_out"][0].reshape(16, 128, 8, 128).transpose(2, 1, 0, 3).reshape(8, 128, 2048)
    i["w_k"] = _lhs_blocks(a["w_kv"][:, :768])
    i["w_v"] = a["w_kv"][:, 768:].reshape(8, 128, 3, 256).transpose(2, 1, 0, 3).reshape(3, 128, 2048)
    i["w_q"] = _lhs_blocks(a["b_w_q"][0])
    i["w_o"] = a["b_w_o"][0].reshape(6, 128, 8, 128).transpose(1, 2, 0, 3).reshape(128, 3, 2048).transpose(1, 0, 2)
    i["skT"] = a["peer_sub_keys"].transpose(3, 0, 1, 2)
    for n in range(2):
        i[f"peer_q{n}"] = _lhs_blocks(a["peer_w_q"][n])
        i[f"U{n}"] = a["peer_u"][n].reshape(128, 64, 2, 8, 128).transpose(1, 4, 2, 3, 0).reshape(64, 128, 2048)
        i[f"V{n}"] = a["peer_v"][n].reshape(128, 4, 2, 16, 8, 128).transpose(1, 4, 2, 0, 3, 5).reshape(64, 128, 2048)
    for n, w in enumerate((128, 512, 2048)):
        c = a[f"cache_kv_w{w}"]
        i[f"cache{n}"] = c.reshape(8, c.shape[1], 2, 256)
    return i


_OUTS = {"yT": (128, 8, 288), "a_v_prompt": (128, 2048), "a_v_sample": (32, 2048), "kT": (128, 6, 288),
         "v_prompt": (128, 2, 768), "v_sample": (32, 768)}


def kernel(**inputs):
    import concourse.bacc as _bacc
    from concourse.bass_utils import run_bass_kernel_spmd as _run

    laid = {k: np.ascontiguousarray(v) for k, v in _layout({k: np.asarray(v) for k, v in inputs.items()}).items()}
    nc = _bacc.Bacc("TRN2", target_bir_lowering=False, num_devices=1)
    ins = {k: nc.dram_tensor(f"in_{k}", v.shape, mybir.dt.from_np(v.dtype), kind="ExternalInput").ap()
           for k, v in laid.items()}
    outs = {k: nc.dram_tensor(f"out_{k}", s, F32, kind="ExternalOutput").ap() for k, s in _OUTS.items()}
    build(nc, ins, outs)
    r = _run(nc, [{f"in_{k}": v for k, v in laid.items()}], core_ids=[0]).results[0]
    y = r["out_yT"].transpose(2, 1, 0).reshape(288, 1024)
    k = r["out_kT"].transpose(2, 1, 0).reshape(288, 3, 4, 64)
    v = np.concatenate([r["out_v_prompt"].transpose(1, 0, 2).reshape(256, 768), r["out_v_sample"]]).reshape(288, 3, 4, 64)
    kv = np.stack([k, v], axis=1)
    prompt, sample = kv[None, :256], kv[256:].reshape(8, 4, 2, 3, 4, 64)
    return (y[None, :256], y[256:].reshape(8, 4, 1024),
            r["out_a_v_prompt"][None, None], r["out_a_v_sample"].reshape(1, 8, 4, 2048),
            prompt[:, 128:, :, 0], prompt[:, :, :, 1], prompt[:, :, :, 2],
            sample[:, :, :, 0], sample[:, :, :, 1], sample[:, :, :, 2])
```

```python
from contextlib import ExitStack

import numpy as np

import concourse.bass as bass
from concourse import mybir

F32 = mybir.dt.float32
BF16 = mybir.dt.bfloat16
F32R = mybir.dt.float32r
U32 = mybir.dt.uint32
ACT = mybir.ActivationFunctionType
ALU = mybir.AluOpType
AXX = mybir.AxisListType.X

P = 128
D = 1024
DC = D // P
NPROMPT, NB, NS = 256, 8, 4
NSAMP = NB * NS
T = NPROMPT + NSAMP
TILES = [(0, 128), (128, 128), (256, 32)]
EPS = 1e-6
DAV = 2 * D
FC = DAV // P
AG = 8
HP = 16
PH = 8
SH = 2
TOP = 16
NK = 128
NQ = 4
EQ = NK // NQ
GT = 8
NGG = T // GT
NX = 4
GR = NGG // 2
WINDOWS_OF_GATES = [(0, 15), (3, 16), (0, 16), (0, 15)]
LEAD = 2
RH = 3
CREDIT = 3
NG, HPG, HD = 3, 4, 64
WINDOWS = (128, 512, 2048)
DILS = (1, 4, 16)
NHB = NG * HPG
AW = NHB * HD
AC = AW // P
SLOPES = [float(np.float32(2.0 ** (-8.0 * (i + 1) / NHB))) for i in range(NHB)]
CK = [128, 128, 64]
CS = [1, 4, 4]
COFF = [0, 256, 1280]
KV = 2304
SCOLS = sum(CK) + NG * NSAMP
BLK = 2048
R = 4
HBLK = BLK // 2
HI_SLOTS, LO_SLOTS = 4, 2
HI_LEAD = 3
SPLIT = 7 * EQ
CCHUNKS = [(0, 1), (1, 3), (3, 6), (6, 10), (10, 14), (14, 19), (19, 25), (25, 32)]
BIG = -3.0e38

TO_ACT = [("v", 12), ("u", FC), ("q0", HP), ("s0", 9), ("U0", NK),
          ("qb", AC), ("qn", 2), ("k", AC), ("vn", 9), ("sp", 2), ("pp", 20),
          ("q1", HP), ("s1", 9), ("U1", NK)]
TO_DVE = [("na", 1), ("gate", FC), ("wo", DC), ("n0", 1), ("e0", 3), ("V0", NQ * DC),
          ("nb", 1), ("qk", 48), ("sc", 3), ("ps", 24), ("ob", DC), ("n1", 1), ("e1", 3),
          ("V1", NQ * DC), ("nf", 1)]


def due(done, of, q):
    first, last = WINDOWS_OF_GATES[q]
    return min(GR, max(0, (16 * done - first * of) * GR // ((last - first) * of)))


def share(k, of, n):
    return k * n // of


def starts(stages):
    at, out = 0, {}
    for name, n in stages:
        out[name] = at
        at += n
    return out


def build(nc, i, o):
    A0, D0 = starts(TO_ACT), starts(TO_DVE)
    with ExitStack() as ctx:
        def sem(name):
            return ctx.enter_context(nc.semaphore(name))

        cursor = {"at": (nc.sbuf_base + 31) // 32 * 32}

        def at_address(name, at, shape, dt=F32):
            return nc.alloc_sbuf_tensor_at(name, shape, dt, offset=at)

        def place(name, shape, dt=F32):
            at = cursor["at"]
            size = int(np.prod(shape[1:])) * (2 if dt == BF16 else 4)
            cursor["at"] = at + (size + 31) // 32 * 32
            return at_address(name, at, shape, dt), at

        xT, _ = place("xT", [P, DC, T])
        ring, _ = place("ring", [P, R, BLK])
        wide, wide_at = place("wide", [P, 16 * T])
        h_hi = at_address("h_hi", wide_at, [P, DC, T], F32R)
        h_lo = at_address("h_lo", wide_at + 4 * DC * T, [P, DC, T], F32R)
        mid, mid_at = place("mid", [P, 3 * DAV])
        w_hi = at_address("w_hi", mid_at, [P, HI_SLOTS, HBLK], F32R)
        w_lo = at_address("w_lo", mid_at + 4 * HI_SLOTS * HBLK, [P, LO_SLOTS, HBLK], F32R)
        big, big_at = place("big", [P, 2 * EQ * T])
        early_at = big_at + 4 * 5120
        eh_hi = at_address("eh_hi", early_at, [P, DC, T], F32R)
        eh_lo = at_address("eh_lo", early_at + 4 * DC * T, [P, DC, T], F32R)
        ew_hi = at_address("ew_hi", early_at + 8 * DC * T, [P, HI_SLOTS, HBLK], F32R)
        ew_lo = at_address("ew_lo", early_at + 8 * DC * T + 4 * HI_SLOTS * HBLK, [P, LO_SLOTS, HBLK], F32R)
        C_lo = at_address("C_lo", big_at, [P, 2, EQ, T], F32R)
        stat, _ = place("stat", [P, 16])
        warm, _ = place("warm", [P, 8])
        halves, _ = place("halves", [P, 2, 3 * P], BF16)
        parts, _ = place("parts", [P, 3, 3 * P], BF16)
        iota16, _ = place("iota16", [P, NK], BF16)
        iota_top, _ = place("iota_top", [P, TOP])
        ident, _ = place("ident", [P, P])
        ident_r, _ = place("ident_r", [NSAMP, NSAMP], F32R)
        ones, _ = place("ones", [P, P])
        gains, _ = place("gains", [P, 6, DC])
        hots, hots_at = place("hots", [P, 2816])
        work = at_address("work", hots_at, [P, 5632])
        C_hi, shared_at = place("C_hi", [P, EQ, T], F32R)
        cursor["at"] = hots_at + 4 * 5632
        hT, _ = place("hT", [P, DC, T])
        rs, _ = place("rs", [P, 3, T])
        slots, slots_at = place("slots", [P, 3, 3 * P])
        q_lo = at_address("q_lo", slots_at, [NSAMP, AW], F32R)
        skT, _ = place("skT", [P, 2, 2, NK])
        sbias, _ = place("sbias", [P, SCOLS])
        iota, _ = place("iota", [P, P])
        q_hi, _ = place("q_hi", [NSAMP, AW], F32R)
        assert cursor["at"] <= shared_at + 4 * EQ * T
        ps = ctx.enter_context(nc.psum_tensor("ps", [P, 8, 512], F32))

        def view(t, at, *shape, parts=P):
            n = int(np.prod(shape))
            v = t[0:parts, at:at + n]
            if len(shape) == 1:
                return v
            names = "abcd"[:len(shape)]
            return v.rearrange(f"p ({' '.join(names)}) -> p {' '.join(names)}",
                               **{c: s for c, s in zip(names, shape)})

        uT = view(wide, 0, FC, T)
        v = view(mid, 0, 3, DAV)
        vgain = view(big, 0, DAV)
        bsp = view(big, DAV, AG, P)
        bss = view(big, DAV + AG * P, AG, NSAMP)
        wsp = view(big, 3328, AG, P)
        wss = view(big, 4352, AG, NSAMP)
        maskp = view(big, 4608, P)
        masks = view(big, 4736, NSAMP)
        qT = view(wide, 0, HP, T)
        S2 = view(mid, 0, 2, HP * NK)
        Ssam = view(mid, 2 * HP * NK, 2 * SH, NK)
        S = view(big, EQ * T, HP, NK)
        cand = view(big, EQ * T + 2048, PH, TOP * TOP)
        eq = view(big, EQ * T + 4096, PH * TOP, TOP)
        tv = view(work, 0, HP, TOP)
        ti = work[:, 256:512].bitcast(U32).rearrange("p (a b) -> p a b", a=HP)
        tif = view(work, 512, PH, 2, TOP)
        cs = view(work, 768, PH, TOP)
        pos = work[:, 896:1024].bitcast(U32)
        pos12 = work[:, 1024:1280].bitcast(U32).rearrange("p (a b) -> p a b", a=2)
        posf = view(work, 1280, 2, PH * TOP)
        gs = view(work, 1536, 2 * PH + SH, TOP)
        gsum = view(work, 1920, 2 * PH + SH)
        grec = view(work, 1944, 2 * PH + SH)
        eg = view(work, 1968, 3, 3, P)
        hot1 = hots[:, 0:1536].bitcast(BF16).rearrange("p (r t e) -> p r t e", r=RH, t=GT)
        hot2 = hots[:, 1536:2688].bitcast(BF16).rearrange("p (r c t e) -> p r c t e", r=RH, c=3, t=GT)
        here2 = hots[:, 2688:2816].bitcast(BF16).rearrange("p (t e) -> p t e", t=GT)
        C = view(big, 0, 2, EQ, T)
        aq = view(wide, 0, AC, T)
        ak = view(wide, AC * T, AC, T)
        Sk = view(wide, 2 * AC * T, NG, P)
        Ss = view(wide, 2 * AC * T + 384, SCOLS)
        av = view(mid, 0, 3, AW)
        dist = view(mid, 2304, NG, 2, 256)
        Pps = [view(mid, 3840, NG, 256), view(work, 0, NG, 256)]
        PpTs = [view(mid, 4608, 6, P), view(work, 768, 6, P)]
        PsT = view(mid, 5376, 6, P)
        Vc = view(big, 0, NB, KV)
        Kc = view(work, 0, 2, KV)
        prod = view(work, 2 * KV, 16, HD)
        qn = slots[0:NSAMP].rearrange("p a b -> p (a b)")[:, 0:AW]

        landed = [sem(f"landed{r}") for r in range(R)]
        blocks_begun = sem("blocks_begun")
        x_loaded = [sem(f"x_loaded{k}") for k in range(NX)]
        consts_loaded, mix_loaded = sem("consts_loaded"), sem("mix_loaded")
        act_full, act_free = sem("act_full"), sem("act_free")
        dve_full, dve_free = sem("dve_full"), sem("dve_free")
        ones_set = sem("ones_set")
        x_ready = sem("x_ready")
        squares = sem("squares")
        ms_ready, root_ready = sem("ms_ready"), sem("root_ready")
        h_ready = sem("h_ready")
        hi_made, lo_made = sem("hi_made"), sem("lo_made")
        halves_begun = sem("halves_begun")
        ehi_made, elo_made, ehalves_begun = sem("ehi_made"), sem("elo_made"), sem("ehalves_begun")
        eh_hi_made, eh_lo_made = sem("eh_hi_made"), sem("eh_lo_made")
        h_hi_made, h_lo_made = sem("h_hi_made"), sem("h_lo_made")
        C_hi_made, C_lo_made = sem("C_hi_made"), sem("C_lo_made")
        sub_keys_loaded, sbias_loaded = sem("sub_keys_loaded"), sem("sbias_loaded")
        v_square, v_ready, ws_ready, ug_ready = sem("v_square"), sem("v_ready"), sem("ws_ready"), sem("ug_ready")
        exp_in, exp_out = sem("exp_in"), sem("exp_out")
        slot_ready = sem("slot_ready")
        hot_ready = sem("hot_ready")
        gate_full, gate_free = sem("gate_full"), sem("gate_free")
        dstep = sem("dstep")
        q_parts = sem("q_parts")
        samples_full, samples_out = sem("samples_full"), sem("samples_out")
        vc_loaded, dist_loaded = sem("vc_loaded"), sem("dist_loaded")
        k_landed = [sem("k_landed0"), sem("k_landed1")]
        k_used = sem("k_used")
        sm_in, sm_exp, sm_out = sem("sm_in"), sem("sm_exp"), sem("sm_out")
        pp_in, pp_exp, pp_out = sem("pp_in"), sem("pp_exp"), sem("pp_out")
        moved = sem("moved")
        av_saved, kv_saved, out_done = sem("av_saved"), sem("kv_saved"), sem("out_done")

        block = ctx.enter_context(nc.Block())

        @block.sync
        def _(sp):
            for k in range(NX):
                piece = slice(k * DC // NX, (k + 1) * DC // NX)
                sp.dma_start(xT[:, piece, :], i["xT"][:, piece, :]).then_inc(x_loaded[k], 16)
            n = 0
            lo_base = split_end = 0
            for name in ("w_in_v", "w_in_u", "w_out", "peer_q0", "U0", "V0", "w_q", "w_k", "w_v",
                         "w_o", "peer_q1", "U1", "V1"):
                if name.startswith("V"):
                    continue
                src = i[name]
                if name.startswith("U"):
                    vsrc = i["V" + name[1]]
                    per = 64 // NQ
                    order = [(src, 0), (src, per)]
                    for q in range(NQ):
                        order.append((vsrc, q * per))
                        if q + 2 < NQ:
                            order.append((src, (q + 2) * per))
                    for k, (s, b0) in enumerate(order):
                        peel = 1 if k == 1 else 0
                        if peel:
                            first_split = n
                            for r in range(R):
                                sp.wait_ge(blocks_begun, n + r - R + 2)
                                sp.dma_start(ring[:, r, :], s[b0 + r]).then_inc(landed[r], 16)
                        with sp.Fori(peel, per // R) as it:
                            for r in range(R):
                                if k == 0:
                                    sp.wait_ge(blocks_begun, it * R + (n + r - R + 2))
                                else:
                                    sp.wait_ge(lo_made, it * (2 * R) + (lo_base + 2 * (n - first_split + r - R + 1)))
                                sp.dma_start(ring[:, r, :], s[it * R + (b0 + r)]).then_inc(landed[r], 16)
                        n += per
                    lo_base += SPLIT
                    split_end = n
                    continue
                for b in range(src.shape[0]):
                    if n < split_end + R and split_end:
                        sp.wait_ge(lo_made, lo_base + 2 * (n - R + 1 - split_end))
                    elif n >= R:
                        sp.wait_ge(blocks_begun, n - R + 2)
                    sp.dma_start(ring[:, n % R, :], src[b]).then_inc(landed[n % R], 16)
                    n += 1

        @block.gpsimd
        def _(pool):
            pool.memset(ones[:], 1.0).then_inc(ones_set, 1)
            for t, s in ((ident[:], "ident"), (iota[:], "iota"), (gains[:], "gains")):
                pool.dma_start(t, i[s]).then_inc(consts_loaded, 16)
            pool.dma_start(skT[:], i["skT"]).then_inc(sub_keys_loaded, 16)
            pool.dma_start(vgain, i["vgain"].partition_broadcast(P)).then_inc(mix_loaded, 16)
            pool.dma_start(bsp, i["bsp"].partition_broadcast(P)).then_inc(mix_loaded, 16)
            pool.dma_start(bss, i["bss"].partition_broadcast(P)).then_inc(mix_loaded, 16)
            pool.dma_start(wsp, i["wsp"]).then_inc(mix_loaded, 16)
            pool.dma_start(wss[0:NSAMP], i["wss"]).then_inc(mix_loaded, 16)
            pool.dma_start(maskp, i["maskp"]).then_inc(mix_loaded, 16)
            pool.dma_start(masks[0:NSAMP], i["masks"]).then_inc(mix_loaded, 16)
            def early_lower_parts(e0):
                def ring_round(it):
                    for k in range(2 * R):
                        n = e0 + k
                        pool.wait_ge(ehi_made, n + 1 if it is None else it * (2 * R) + (n + 1))
                        if n >= LO_SLOTS or it is not None:
                            begun = n - LO_SLOTS + 2
                            pool.wait_ge(ehalves_begun, begun if it is None else it * (2 * R) + begun)
                        pool.tensor_tensor(ew_lo[:, k % LO_SLOTS, :], ring[:, k // 2, (k % 2) * HBLK:(k % 2 + 1) * HBLK],
                                           ew_hi[:, k % HI_SLOTS, :], ALU.subtract).then_inc(elo_made, 1)

                ring_round(None)
                with pool.Fori(1, 2) as it:
                    ring_round(it)

            early_lower_parts(0)
            pool.wait_ge(v_ready, 1)
            pool.dma_start(o["a_v_prompt"], v[:, 1, :]).then_inc(av_saved, 16)
            pool.dma_start(o["a_v_sample"], v[0:NSAMP, 2, :]).then_inc(av_saved, 16)

            def lower_parts(layer):
                pool.wait_ge(h_hi_made, layer + 1)
                pool.tensor_tensor(h_lo[:], hT[:], h_hi[:], ALU.subtract).then_inc(h_lo_made, 1)

                def ring_round(it):
                    for k in range(2 * R):
                        n = layer * SPLIT + k
                        pool.wait_ge(hi_made, n + 1 if it is None else it * (2 * R) + (n + 1))
                        if n >= LO_SLOTS or it is not None:
                            begun = n - LO_SLOTS + 2
                            pool.wait_ge(halves_begun, begun if it is None else it * (2 * R) + begun)
                        pool.tensor_tensor(w_lo[:, k % LO_SLOTS, :], ring[:, k // 2, (k % 2) * HBLK:(k % 2 + 1) * HBLK],
                                           w_hi[:, k % HI_SLOTS, :], ALU.subtract).then_inc(lo_made, 1)

                ring_round(None)
                with pool.Fori(1, SPLIT // (2 * R)) as it:
                    ring_round(it)

            early_lower_parts(16)
            lower_parts(0)
            pool.wait_ge(x_ready, 2)
            pool.dma_start(skT[:], i["skT"]).then_inc(sub_keys_loaded, 16)
            pool.dma_start(sbias[:], i["sbias"]).then_inc(sbias_loaded, 16)
            pool.dma_start(dist, i["dist"]).then_inc(dist_loaded, 16)
            cache = [i["cache0"], i["cache1"], i["cache2"]]

            def load_cache(dst, b, which, done):
                for g in range(NG):
                    n, s = CK[g], CS[g]
                    rows = cache[g][b].rearrange("(r s) k c -> r s k c", r=n)[:, 0:s, which, :]
                    d = dst[0:n, COFF[g]:COFF[g] + s * 256].rearrange("p (s c) -> p s c", s=s)
                    pool.dma_start(d, rows).then_inc(done, 16)

            for b in range(NB):
                if b >= 2:
                    pool.wait_ge(k_used, b - 1)
                load_cache(Kc[:, b % 2, :], b, 0, k_landed[b % 2])
                load_cache(Vc[:, b, :], b, 1, vc_loaded)
            pool.wait_ge(act_free, A0["sp"])
            pool.dma_start(o["kT"], ak).then_inc(kv_saved, 16)
            pool.dma_start(o["v_prompt"], av[:, 0:2, :]).then_inc(kv_saved, 16)
            pool.dma_start(o["v_sample"], av[0:NSAMP, 2, :]).then_inc(kv_saved, 16)
            early_lower_parts(32)
            lower_parts(1)
            for c in (0, DC // 2):
                pool.wait_ge(h_ready, 5 * DC + c + DC // 2)
                pool.dma_start(o["yT"][:, c:c + DC // 2, :], hT[:, c:c + DC // 2, :]).then_inc(out_done, 16)
            pool.wait_ge(av_saved, 16 * 2)
            pool.wait_ge(kv_saved, 16 * 3)
            pool.wait_ge(out_done, 16 * 2)

        @block.tensor
        def _(pe):
            state = {"block": 0, "half": 0}

            def arrived(n, i4=None, rounds=0):
                want = 16 * (n // R + 1)
                pe.wait_ge(landed[n % R], want if i4 is None else i4 * (16 * rounds) + want)
                return n % R

            def act_bank(stage, k):
                if k < 4:
                    if A0[stage] > 0:
                        pe.wait_ge(act_free, A0[stage])
                else:
                    pe.wait_ge(act_free, A0[stage] + k - 3)
                return k % 4

            def dve_bank(stage, k):
                if k < 4:
                    if D0[stage] > 0:
                        pe.wait_ge(dve_free, D0[stage])
                else:
                    pe.wait_ge(dve_free, D0[stage] + k - 3)
                return 4 + k % 4

            def mean_square(stage, nth):
                b = dve_bank(stage, 0)
                for c in range(DC):
                    pe.wait_ge(squares, (nth - 1) * NX + c * NX // DC + 1)
                    last = pe.matmul(ps[:, b, 0:T], ones[:], hT[:, c, :], start=(c == 0), stop=(c == DC - 1))
                last.then_inc(dve_full, 1)

            def project_split(stage, e0, fresh):
                pe.wait_ge(act_free, A0[stage])

                def eight(it):
                    for h in range(8):
                        pe.wait_ge(elo_made, e0 + h + 1 if it is None else it * 8 + (e0 + h + 1))
                        if it is not None or h >= 4:
                            free = A0[stage] + h - 3
                            pe.wait_ge(act_free, free if it is None else it * 8 + free)
                        for c in range(DC):
                            if it is None and h == 0:
                                pe.wait_ge(eh_lo_made, fresh + c + 1)
                            at = slice(c * P, (c + 1) * P)
                            out = ps[:, h % 4, 0:T]
                            one = pe.matmul(out, ew_hi[:, h % HI_SLOTS, at], eh_hi[:, c, :], start=(c == 0), stop=False)
                            two = pe.matmul(out, ew_hi[:, h % HI_SLOTS, at], eh_lo[:, c, :], start=False, stop=False)
                            three = pe.matmul(out, ew_lo[:, h % LO_SLOTS, at], eh_hi[:, c, :],
                                              start=False, stop=(c == DC - 1))
                            if c == 0:
                                if h % 2 == 0:
                                    one.then_inc(blocks_begun, 1)
                                two.then_inc(ehalves_begun, 1)
                            if c == DC - 1:
                                three.then_inc(act_full, 1)

                eight(None)
                with pe.Fori(1, 2) as it:
                    eight(it)
                state["block"] += 8

            def project(stage, nblocks, fresh=None):
                for bl in range(nblocks):
                    r = arrived(state["block"])
                    for j in range(2):
                        b = act_bank(stage, 2 * bl + j)
                        for c in range(DC):
                            if fresh is not None and bl == 0 and j == 0:
                                pe.wait_ge(h_ready, fresh + c + 1)
                            at = (j * DC + c) * P
                            last = pe.matmul(ps[:, b, 0:T], ring[:, r, at:at + P], hT[:, c, :],
                                             start=(c == 0), stop=(c == DC - 1))
                            if c == 0 and j == 0:
                                last.then_inc(blocks_begun, 1)
                        last.then_inc(act_full, 1)
                    state["block"] += 1

            pe.wait_ge(ones_set, 1)
            mean_square("na", 1)
            for fg in range(4):
                n0 = state["block"]
                rr = [arrived(n0), arrived(n0 + 1)]
                for m, (t0, tn) in enumerate(TILES):
                    b = act_bank("v", 3 * fg + m)
                    for c in range(DC):
                        if fg == 0 and m == 0:
                            pe.wait_ge(h_ready, c + 1)
                        last = pe.matmul(ps[0:tn, b, :], hT[:, c, t0:t0 + tn],
                                         ring[:, rr[c // 4], (c % 4) * 512:(c % 4 + 1) * 512],
                                         start=(c == 0), stop=(c == DC - 1))
                        if (m, c) in ((0, 0), (2, 4)):
                            last.then_inc(blocks_begun, 1)
                    last.then_inc(act_full, 1)
                state["block"] += 2
            project_split("u", 0, 0)
            pe.wait_ge(v_ready, 1)
            pe.wait_ge(ws_ready, 1)
            for c in range(FC):
                b = dve_bank("gate", c)
                g = c * P // 256
                for m, (t0, tn) in enumerate(TILES):
                    w = wsp[:, g, :] if m < 2 else wss[0:NSAMP, g, :]
                    last = pe.matmul(ps[:, b, t0:t0 + tn], v[0:tn, m, c * P:(c + 1) * P], w, start=True, stop=True)
                last.then_inc(dve_full, 1)
            for c in range(DC):
                r = arrived(state["block"])
                b = dve_bank("wo", c)
                for f in range(FC):
                    if c == 0:
                        pe.wait_ge(ug_ready, f + 1)
                    last = pe.matmul(ps[:, b, 0:T], ring[:, r, f * P:(f + 1) * P], uT[:, f, :],
                                     start=(f == 0), stop=(f == FC - 1))
                    if f == 0:
                        last.then_inc(blocks_begun, 1)
                last.then_inc(dve_full, 1)
                state["block"] += 1

            def peer(layer):
                mean_square(f"n{layer}", 2 + 2 * layer)
                project_split(f"q{layer}", 16 * (layer + 1), (layer + 1) * DC)
                pe.wait_ge(act_free, A0[f"s{layer}"])
                pe.wait_ge(sub_keys_loaded, 16 * (layer + 1))
                for m, (t0, tn) in enumerate(TILES):
                    for g4 in range(4):
                        if m < 2 or g4 == 0:
                            b = act_bank(f"s{layer}", 4 * m + g4)
                        rows = slice(0, P) if m < 2 else slice(32 * g4, 32 * g4 + tn)
                        for j in range(4):
                            hp = 4 * g4 + j
                            last = pe.matmul(ps[rows, b, j * NK:(j + 1) * NK], qT[:, hp, t0:t0 + tn],
                                             skT[:, layer, hp % 2, :], start=True, stop=True)
                        if m < 2 or g4 == 3:
                            last.then_inc(act_full, 1)

                def slot_transposes():
                    for m in range(3):
                        pe.wait_ge(slot_ready, layer + 1)
                        b = dve_bank(f"e{layer}", m)
                        for a in range(3):
                            if m < 2:
                                last = pe.transpose(ps[:, b, a * P:(a + 1) * P], eg[:, m, a, :], ident[:])
                                continue
                            for g4 in range(4):
                                rows = slice(32 * g4, 32 * g4 + 32)
                                last = pe.matmul(ps[rows, b, a * 32:(a + 1) * 32], eg[rows, m, a, 0:32],
                                                 ident[rows, rows], start=True, stop=True)
                        last.then_inc(dve_full, 1)

                def gate_groups(q, done, of, it):
                    if q is None:
                        return
                    nth = layer * NQ + q
                    for j in range(due(done, of, q), due(done + 1, of, q)):
                        pe.wait_ge(hot_ready, it * GR + (nth * (NGG + LEAD) + j + 1))
                        pe.wait_ge(gate_free, it * GR + (nth * NGG + j - 1 + CREDIT))
                        for t in range(GT):
                            for c in range(3):
                                g = pe.matmul(ps[:, 6 + j % 2, t * EQ:(t + 1) * EQ], hot1[:, j % RH, t, :],
                                              hot2[:, j % RH, c, t, :], start=(c == 0), stop=(c == 2))
                        g.then_inc(gate_full, 1)

                def up_whole(q):
                    n0 = state["block"]
                    k0 = A0[f"U{layer}"] + q * EQ
                    pe.wait_ge(act_free, A0[f"U{layer}"])
                    with pe.Fori(0, 2) as it:
                        for bl in range(8):
                            r = arrived(n0 + bl, it, 2)
                            for j in range(2 * bl, 2 * bl + 2):
                                pe.wait_ge(act_free, it * 16 + (k0 + j - 3))
                                for c in range(DC):
                                    at = ((j % 2) * DC + c) * P
                                    last = pe.matmul(ps[:, j % 4, 0:T], ring[:, r, at:at + P], hT[:, c, :],
                                                     start=(c == 0), stop=(c == DC - 1))
                                    if c == 0 and j % 2 == 0:
                                        last.then_inc(blocks_begun, 1)
                                last.then_inc(act_full, 1)
                    state["block"] += EQ // 2

                def product(out, h, tile, hi, lo, start, stop):
                    at = slice(tile * P, (tile + 1) * P)
                    one = pe.matmul(out, w_hi[:, h % HI_SLOTS, at], hi, start=start, stop=False)
                    two = pe.matmul(out, w_hi[:, h % HI_SLOTS, at], lo, start=False, stop=False)
                    if tile == 0:
                        if h % 2 == 0:
                            one.then_inc(blocks_begun, 1)
                        two.then_inc(halves_begun, 1)
                    return pe.matmul(out, w_lo[:, h % LO_SLOTS, at], hi, start=False, stop=stop)

                def up(q, gates=None):
                    h0 = state["half"]
                    k0 = A0[f"U{layer}"] + q * EQ
                    with pe.Fori(0, 2) as it:
                        for h in range(16):
                            pe.wait_ge(lo_made, it * 16 + (h0 + h + 1))
                            pe.wait_ge(act_free, it * 16 + (k0 + h - 3))
                            for c in range(DC):
                                last = product(ps[:, h % 4, 0:T], h, c, h_hi[:, c, :], h_lo[:, c, :],
                                               c == 0, c == DC - 1)
                                if c == DC - 1:
                                    last.then_inc(act_full, 1)
                                gate_groups(gates, h * DC + c, 16 * DC, it)
                    state["half"] += EQ
                    state["block"] += EQ // 2

                def down(q, gates=None):
                    h0 = state["half"]
                    k0 = D0[f"V{layer}"] + q * DC
                    c0 = (layer * NQ + q) * len(CCHUNKS)
                    with pe.Fori(0, 2) as it:
                        for h in range(16):
                            dc = h // 4
                            if h % 4 == 0:
                                pe.wait_ge(dve_free, it * 4 + (k0 + dc - 1))
                            pe.wait_ge(lo_made, it * 16 + (h0 + h + 1))
                            for t in range(8):
                                e = (h % 4) * 8 + t
                                for k, (e0, _) in enumerate(CCHUNKS):
                                    if dc == 0 and e == e0:
                                        pe.wait_ge(C_lo_made, c0 + k + 1)
                                last = product(ps[:, 4 + dc % 2, 0:T], h, t, C_hi[:, e, :], C_lo[:, q % 2, e, :],
                                               e == 0, e == EQ - 1)
                                if e == EQ - 1:
                                    last.then_inc(dve_full, 1)
                                gate_groups(gates, h * 8 + t, 128, it)
                    state["half"] += EQ
                    state["block"] += EQ // 2

                up_whole(0)
                slot_transposes()
                pe.wait_ge(dve_free, D0[f"V{layer}"])
                pe.wait_ge(h_lo_made, layer + 1)
                up(1, 0)
                down(0, 1)
                up(2)
                down(1, 2)
                up(3)
                down(2, 3)
                down(3)

            peer(0)

            mean_square("nb", 3)
            project("qb", 3, fresh=2 * DC)
            for k in range(2):
                b = act_bank("qn", k)
                pe.wait_ge(act_free, A0["qn"])
                for j in range(3):
                    last = pe.transpose(ps[0:NSAMP, b, j * P:(j + 1) * P], aq[:, 3 * k + j, NPROMPT:T], ident[:])
                last.then_inc(act_full, 1)

            def spread_queries(first, last_):
                for n in range(first, last_):
                    b_, g, pr = n // 6, n // 2 % 3, n % 2
                    b = dve_bank("qk", n)
                    for j in range(2):
                        tok = NS * b_ + 2 * pr + j
                        for k, part in enumerate((q_hi, q_lo)):
                            last = pe.matmul(ps[:, b, j * 256:(j + 1) * 256],
                                             ident_r[:, tok:tok + 1].broadcast_to((NSAMP, P)),
                                             part[:, g * 256:(g + 1) * 256], start=(k == 0), stop=(k == 1))
                    last.then_inc(dve_full, 1)

            pe.wait_ge(q_parts, 1)
            outputs = AC + 9
            for bl in range(3):
                r = arrived(state["block"])
                for j in range(2):
                    n = 2 * bl + j
                    b = act_bank("k", n)
                    for c in range(DC):
                        if n == 0:
                            pe.wait_ge(h_ready, 3 * DC + c + 1)
                        at = (j * DC + c) * P
                        last = pe.matmul(ps[:, b, 0:T], ring[:, r, at:at + P], hT[:, c, :],
                                         start=(c == 0), stop=(c == DC - 1))
                        if c == 0 and j == 0:
                            last.then_inc(blocks_begun, 1)
                    last.then_inc(act_full, 1)
                    spread_queries(share(n, outputs, 48), share(n + 1, outputs, 48))
                state["block"] += 1
            for fg in range(3):
                r = arrived(state["block"])
                for m, (t0, tn) in enumerate(TILES):
                    n = 3 * fg + m
                    b = act_bank("vn", n)
                    for c in range(DC):
                        last = pe.matmul(ps[0:tn, b, 0:256], hT[:, c, t0:t0 + tn], ring[:, r, c * 256:(c + 1) * 256],
                                         start=(c == 0), stop=(c == DC - 1))
                        if m == 0 and c == 0:
                            last.then_inc(blocks_begun, 1)
                    last.then_inc(act_full, 1)
                    spread_queries(share(AC + n, outputs, 48), share(AC + n + 1, outputs, 48))
                state["block"] += 1
            pe.wait_ge(k_used, NB)
            b = dve_bank("sc", 0)
            at = 0
            for g in range(NG):
                last = pe.transpose(ps[:, b, at:at + CK[g]], Sk[0:CK[g], g, :], ident[0:CK[g], 0:CK[g]])
                at += CK[g]
            last.then_inc(dve_full, 1)
            for par in range(2):
                b = dve_bank("sc", 1 + par)
                for h in (par, par + 2):
                    for g in range(NG):
                        row = par * HD
                        last = pe.matmul(ps[32 * h:32 * h + 32, b, g * NSAMP:(g + 1) * NSAMP],
                                         aq[row:row + HD, 2 * g + h // 2, NPROMPT:T],
                                         ak[row:row + HD, 2 * g + h // 2, NPROMPT:T], start=True, stop=True)
                last.then_inc(dve_full, 1)

            def prompt_scores(u):
                h, m = u // 2, u % 2
                row = (h % 2) * HD
                for g in range(NG):
                    b = dve_bank("ps", 3 * u + g)
                    pe.matmul(ps[:, b, 0:P * (m + 1)], aq[row:row + HD, 2 * g + h // 2, m * P:(m + 1) * P],
                              ak[row:row + HD, 2 * g + h // 2, 0:P * (m + 1)],
                              start=True, stop=True).then_inc(dve_full, 1)

            prompt_scores(0)
            prompt_scores(1)
            pe.wait_ge(sm_out, 1)
            b = act_bank("sp", 0)
            at = 0
            for g in range(NG):
                last = pe.transpose(ps[0:CK[g], b, g * P:(g + 1) * P], Ss[:, at:at + CK[g]], ident[:])
                at += CK[g]
            last.then_inc(act_full, 1)
            b = act_bank("sp", 1)
            for g in range(NG):
                last = pe.transpose(ps[0:NSAMP, b, g * P:(g + 1) * P], Ss[:, at:at + NSAMP], ident[:])
                at += NSAMP
            last.then_inc(act_full, 1)

            def sample_products():
                for g in range(NG):
                    for pr in range(2):
                        dst = ps[:, 3, (g * 2 + pr) * 64:(g * 2 + pr + 1) * 64]
                        dst3 = dst.rearrange("p (j t) -> p j t", j=2)
                        yield pe.matmul(dst, av[0:NSAMP, 2, g * 256 + pr * P:g * 256 + (pr + 1) * P],
                                        PsT[0:NSAMP, 3 + g, pr * 64:(pr + 1) * 64], start=True, stop=False,
                                        skip_group_check=True)
                        prob = PsT[0:CK[g], g, pr * 64:(pr + 1) * 64].rearrange("p (j t) -> p j t", j=2)
                        for b_ in range(NB):
                            for s in range(CS[g]):
                                w = NS // CS[g]
                                t0 = NS * b_ + s * w
                                at = COFF[g] + s * 256 + pr * P
                                yield pe.matmul(dst3[:, :, t0:t0 + w], Vc[0:CK[g], b_, at:at + P],
                                                prob[:, :, t0:t0 + w], start=False,
                                                stop=(b_ == NB - 1 and s == CS[g] - 1), skip_group_check=True)

            pe.wait_ge(act_free, A0["pp"])
            pe.wait_ge(vc_loaded, 16 * NG * NB)
            sample = sample_products()
            nsample = 2 * sum(1 + NB * s for s in CS)

            def sample_share(k):
                last = None
                for _ in range(share(k, 16, nsample), share(k + 1, 16, nsample)):
                    last = next(sample)
                return last

            def unit_bank(kk):
                if kk >= 3:
                    pe.wait_ge(act_free, A0["pp"] + kk - 2)
                return kk % 3

            kk = 0
            for u in range(8):
                h, m = u // 2, u % 2
                if u + 2 < 8:
                    prompt_scores(u + 2)
                sample_share(2 * u)
                pe.wait_ge(pp_out, u + 1)
                for half in range(m + 1):
                    b = unit_bank(kk)
                    kk += 1
                    for g in range(NG):
                        last = pe.transpose(ps[:, b, g * P:(g + 1) * P], Pps[m][:, g, half * P:(half + 1) * P], ident[:])
                    last.then_inc(act_full, 1)
                last = sample_share(2 * u + 1)
                if u == 7:
                    last.then_inc(samples_full, 1)
                pe.wait_ge(act_free, A0["pp"] + kk)
                b = unit_bank(kk)
                kk += 1
                row = (h % 2) * HD
                for g in range(NG):
                    f0 = g * 256 + h * HD
                    for half in range(m + 1):
                        last = pe.matmul(ps[row:row + HD, b, g * P:(g + 1) * P], av[:, half, f0:f0 + HD],
                                         PpTs[m][:, half * 3 + g, :], start=(half == 0), stop=(half == m))
                last.then_inc(act_full, 1)
            pe.wait_ge(act_free, A0["q1"])
            pe.wait_ge(samples_out, 1)
            for c in range(DC):
                b = dve_bank("ob", c)
                for f in range(AC):
                    k = c * AC + f
                    if k % 16 == 0:
                        r = arrived(state["block"])
                    last = pe.matmul(ps[:, b, 0:T], ring[:, r, (k % 16) * P:(k % 16 + 1) * P], hT[:, f, :],
                                     start=(f == 0), stop=(f == AC - 1))
                    if k % 16 == 0:
                        last.then_inc(blocks_begun, 1)
                        state["block"] += 1
                last.then_inc(dve_full, 1)
            peer(1)
            mean_square("nf", 5)

        early_block = [8, 8 + 8 + DC, 8 + 8 + DC + 8 + 8 * EQ // 2 + 12]
        first_split_block = [8 + 8 + DC + 8 + EQ // 2]
        first_split_block.append(first_split_block[0] + SPLIT // 2 + 3 + 3 + 3 + 3 + 8 + EQ // 2)

        @block.scalar
        def _(act):
            def full(stage, k):
                act.wait_ge(act_full, A0[stage] + k + 1)
                return k % 4

            def norm_part(nth):
                if nth > 1:
                    act.wait_ge(x_ready, nth - 1)
                for k in range(NX):
                    if nth == 1:
                        act.wait_ge(x_loaded[k], 16)
                    piece = slice(k * DC // NX, (k + 1) * DC // NX)
                    act.activation(hT[:, piece, :], xT[:, piece, :], ACT.Square).then_inc(squares, 1)
                act.activation(warm[:, nth - 1:nth], ones[:, 0:1], ACT.Sqrt)
                act.wait_ge(ms_ready, nth if nth == 1 else nth + 1)
                act.activation(rs[:, 1, :], rs[:, 0, :], ACT.Sqrt).then_inc(root_ready, 1)

            def early_upper(e0, k):
                bl = early_block[e0 // 16] + k // 2
                act.wait_ge(landed[bl % R], 16 * (bl // R + 1))
                if e0 + k >= HI_SLOTS:
                    act.wait_ge(ehalves_begun, e0 + k - HI_SLOTS + 2)
                act.activation(ew_hi[:, k % HI_SLOTS, :], ring[:, bl % R, (k % 2) * HBLK:(k % 2 + 1) * HBLK],
                               ACT.Copy).then_inc(ehi_made, 1)

            def early_outputs(stage, e0, dst, function, first=0, last=16):
                for c in range(first, last):
                    if c + HI_LEAD < 16:
                        early_upper(e0, c + HI_LEAD)
                    act.wait_ge(act_full, A0[stage] + c + 1)
                    act.activation(dst[:, c, :], ps[:, c % 4, 0:T], function).then_inc(act_free, 1)

            def early_h(chunks_before):
                for c in range(DC):
                    act.wait_ge(h_ready, chunks_before + c + 1)
                    act.activation(eh_hi[:, c, :], hT[:, c, :], ACT.Copy).then_inc(eh_hi_made, 1)

            act.wait_ge(ones_set, 1)
            norm_part(1)
            early_h(0)
            for fg in range(4):
                for m, (t0, tn) in enumerate(TILES):
                    b = full("v", 3 * fg + m)
                    act.activation(v[0:tn, m, fg * 512:(fg + 1) * 512], ps[0:tn, b, :],
                                   ACT.Gelu_apprx_tanh).then_inc(act_free, 1)
            for k in range(HI_LEAD):
                early_upper(0, k)
            act.wait_ge(act_free, A0["u"])
            act.wait_ge(moved, 1)
            for m, (t0, tn) in enumerate(TILES):
                junk = work[0:tn, m * DAV:(m + 1) * DAV] if m < 2 else view(big, 16384, DAV, parts=tn)
                last = act.activation(junk, v[0:tn, m, :], ACT.Square, accum_out=stat[0:tn, m:m + 1])
            last.then_inc(v_square, 1)
            early_outputs("u", 0, uT, ACT.Gelu_apprx_tanh, 0, 2)
            act.wait_ge(ms_ready, 2)
            act.activation(stat[:, 6:9], stat[:, 3:6], ACT.Sqrt).then_inc(root_ready, 1)
            early_outputs("u", 0, uT, ACT.Gelu_apprx_tanh, 2)

            def peer(layer):
                norm_part(2 + 2 * layer)
                e0 = 16 * (layer + 1)
                for k in range(HI_LEAD):
                    early_upper(e0, k)
                early_h((1 + 3 * layer) * DC)
                if layer == 1:
                    act.wait_ge(kv_saved, 16 * 3)
                early_outputs(f"q{layer}", e0, qT, ACT.Copy)

                block0 = first_split_block[layer]

                def upper_part(k, it=None, per=16):
                    n = layer * SPLIT + k
                    bl = block0 + k // 2
                    want = 16 * (bl // R + 1)
                    act.wait_ge(landed[bl % R], want if it is None else it * (2 * per) + want)
                    if n >= HI_SLOTS or it is not None:
                        begun = n - HI_SLOTS + 2
                        act.wait_ge(halves_begun, begun if it is None else it * per + begun)
                    act.activation(w_hi[:, k % HI_SLOTS, :], ring[:, bl % R, (k % 2) * HBLK:(k % 2 + 1) * HBLK],
                                   ACT.Copy).then_inc(hi_made, 1)

                def gates_applied(q):
                    act.wait_ge(gate_free, (layer * NQ + q + 1) * NGG + CREDIT)
                    if q:
                        act.wait_ge(dve_full, D0[f"V{layer}"] + q * DC)

                def upper_C(q, pieces):
                    for e0, e1 in pieces:
                        act.activation(C_hi[:, e0:e1, :], C[:, q % 2, e0:e1, :], ACT.Copy).then_inc(C_hi_made, 1)

                def up(nth, q, split=None):
                    k0 = nth * EQ + HI_LEAD
                    u0 = A0[f"U{layer}"] + q * EQ

                    def step(h, it=None):
                        upper_part(k0 + h, it, 8)
                        act.wait_ge(act_full, u0 + h + 1 if it is None else it * 8 + (u0 + h + 1))
                        e = h if it is None else it * 8 + h
                        act.activation(C[:, q % 2, e, :], ps[:, h % 4, 0:T], ACT.Gelu_apprx_tanh).then_inc(act_free, 1)

                    if split is not None:
                        gates_applied(split)
                    for h in range(8):
                        step(h)
                        if split is not None:
                            upper_C(split, CCHUNKS[h:h + 1])
                    with act.Fori(1, EQ // 8) as it:
                        for h in range(8):
                            step(h, it)

                def down(nth, split=None):
                    k0 = nth * EQ + HI_LEAD
                    n = 0
                    if split is not None:
                        gates_applied(split)
                        upper_C(split, CCHUNKS[:4])
                        upper_part(k0)
                        upper_C(split, CCHUNKS[4:])
                        n = 1
                    for k in range(n, 8):
                        upper_part(k0 + k)
                    left = min(EQ, SPLIT - k0)
                    with act.Fori(1, left // 8) as it:
                        for k in range(8):
                            upper_part(k0 + k, it, 8)
                    for k in range(left // 8 * 8, left):
                        upper_part(k0 + k)

                if layer == 0:
                    act.wait_ge(av_saved, 16 * 2)
                for m in range(2):
                    for g4 in range(4):
                        b = full(f"s{layer}", 4 * m + g4)
                        act.activation(S2[:, m, g4 * 512:(g4 + 1) * 512], ps[:, b, :], ACT.Copy).then_inc(act_free, 1)
                b = full(f"s{layer}", 8)
                act.activation(Ssam.rearrange("p a b -> p (a b)"), ps[:, b, :], ACT.Copy).then_inc(act_free, 1)
                act.activation(h_hi[:], hT[:], ACT.Copy).then_inc(h_hi_made, 1)
                k0 = A0[f"U{layer}"]
                with act.Fori(0, EQ // 8) as it:
                    for j in range(8):
                        act.wait_ge(act_full, it * 8 + (k0 + j + 1))
                        act.activation(C[:, 0, it * 8 + j, :], ps[:, j % 4, 0:T],
                                       ACT.Gelu_apprx_tanh).then_inc(act_free, 1)
                act.wait_ge(exp_in, layer + 1)
                act.activation(gs, gs, ACT.Exp).then_inc(exp_out, 1)
                for k in range(HI_LEAD):
                    upper_part(k)
                up(0, 1)
                down(1, split=0)
                up(2, 2, split=1)
                down(3)
                up(4, 3, split=2)
                down(5)
                down(6, split=3)

            peer(0)

            norm_part(3)
            for c in range(AC):
                b = full("qb", c)
                act.activation(aq[:, c, :], ps[:, b, 0:T], ACT.Copy, scale=HD ** -0.5).then_inc(act_free, 1)
            act.activation(ident_r[:], ident[0:NSAMP, 0:NSAMP], ACT.Copy)
            for k in range(2):
                b = full("qn", k)
                act.activation(q_hi[:, k * 384:(k + 1) * 384], ps[0:NSAMP, b, 0:384], ACT.Copy)
                act.activation(qn[:, k * 384:(k + 1) * 384], ps[0:NSAMP, b, 0:384], ACT.Copy).then_inc(act_free, 1)
            for c in range(AC):
                b = full("k", c)
                act.activation(ak[:, c, :], ps[:, b, 0:T], ACT.Copy).then_inc(act_free, 1)
            for fg in range(3):
                for m, (t0, tn) in enumerate(TILES):
                    b = full("vn", 3 * fg + m)
                    act.activation(av[0:tn, m, fg * 256:(fg + 1) * 256], ps[0:tn, b, 0:256],
                                   ACT.Copy).then_inc(act_free, 1)
            act.wait_ge(sm_in, 1)
            act.activation(Ss, Ss, ACT.Exp, bias=stat[:, 9:10], accum_out=stat[:, 10:11]).then_inc(sm_exp, 1)

            def unit_exp(u):
                m = u % 2
                act.wait_ge(pp_in, u + 1)
                act.activation(Pps[m][:, :, 0:P * (m + 1)], Pps[m][:, :, 0:P * (m + 1)], ACT.Exp,
                               bias=stat[:, 11 + 2 * m:12 + 2 * m],
                               accum_out=stat[:, 12 + 2 * m:13 + 2 * m]).then_inc(pp_exp, 1)

            unit_exp(0)
            b = full("sp", 0)
            act.activation(PsT[:, 0:2, :].rearrange("p a b -> p (a b)"), ps[:, b, 0:256], ACT.Copy)
            act.activation(PsT[0:CK[2], 2, :], ps[0:CK[2], b, 256:384], ACT.Copy).then_inc(act_free, 1)
            b = full("sp", 1)
            act.activation(PsT[0:NSAMP, 3:6, :].rearrange("p a b -> p (a b)"), ps[0:NSAMP, b, 0:384],
                           ACT.Copy).then_inc(act_free, 1)
            kk = 0
            for u in range(8):
                h, m = u // 2, u % 2
                row = (h % 2) * HD
                if u + 1 < 8:
                    unit_exp(u + 1)
                for half in range(m + 1):
                    act.wait_ge(act_full, A0["pp"] + kk + 1)
                    act.activation(PpTs[m][:, 3 * half:3 * half + 3, :].rearrange("p a b -> p (a b)"),
                                   ps[:, kk % 3, 0:384], ACT.Copy).then_inc(act_free, 1)
                    kk += 1
                act.wait_ge(act_full, A0["pp"] + kk + 1)
                dst = hT[row:row + HD, :, m * P:(m + 1) * P]
                for g in range(NG):
                    last = act.activation(dst[:, 2 * g + h // 2, :], ps[row:row + HD, kk % 3, g * P:(g + 1) * P], ACT.Copy)
                last.then_inc(act_free, 1)
                kk += 1
            act.wait_ge(samples_full, 1)
            o3 = ps[:, 3, 0:384].rearrange("p (c j t) -> p c j t", c=AC, j=2)
            act.activation(hT[0:HD, 0:AC, NPROMPT:T], o3[0:HD, :, 0, :], ACT.Copy)
            act.activation(hT[HD:P, 0:AC, NPROMPT:T], o3[HD:P, :, 1, :], ACT.Copy).then_inc(samples_out, 1)
            peer(1)
            norm_part(5)

        @block.vector
        def _(dve):
            count = {"n": 0, "it": None, "per": 0}

            def step(ins):
                count["n"] += 1
                ins.then_inc(dstep, 1)

            def last_step():
                it = count["it"]
                dve.wait_ge(dstep, count["n"] if it is None else it * count["per"] + count["n"])

            def link(ins):
                step(ins)
                last_step()

            def loop(n, per, body):
                n0 = count["n"]
                with dve.Fori(0, n) as it:
                    count["it"], count["per"] = it, per
                    body(it)
                assert count["n"] == n0 + per, (count["n"] - n0, per)
                count["it"], count["n"] = None, n0 + n * per

            def full(stage, k):
                dve.wait_ge(dve_full, D0[stage] + k + 1)
                return 4 + k % 4

            def newton(r, ms, tmp):
                link(dve.tensor_tensor(tmp, r, r, ALU.mult))
                link(dve.tensor_tensor(tmp, tmp, ms, ALU.mult))
                link(dve.tensor_scalar(tmp, tmp, -0.5, 1.5, ALU.mult, ALU.add))
                link(dve.tensor_tensor(r, r, tmp, ALU.mult))

            def norm(stage, nth_root, gain, split=None):
                b = full(stage, 0)
                dve.tensor_scalar(rs[:, 0, :], ps[:, b, 0:T], 1.0 / D, EPS, ALU.mult, ALU.add).then_inc(dve_free, 1)
                dve.wait_ge(dve_free, D0[stage] + 1)
                dve.engine_nop().then_inc(ms_ready, 1)
                dve.wait_ge(root_ready, nth_root)
                link(dve.reciprocal(rs[:, 2, :], rs[:, 1, :]))
                newton(rs[:, 2, :], rs[:, 0, :], rs[:, 1, :])
                scaled(gain, split)

            def early_lower_h(before, c):
                dve.wait_ge(eh_hi_made, before + c + 1)
                dve.tensor_tensor(eh_lo[:, c, :], hT[:, c, :], eh_hi[:, c, :], ALU.subtract).then_inc(eh_lo_made, 1)

            def scaled(gain, split=None):
                for c in range(DC):
                    if split is not None and c >= 2:
                        early_lower_h(split, c - 2)
                    dve.scalar_tensor_tensor(out=hT[:, c, :], in0=xT[:, c, :], scalar=gains[:, gain, c:c + 1],
                                             in1=rs[:, 2, :], op0=ALU.mult, op1=ALU.mult).then_inc(h_ready, 1)
                if split is not None:
                    early_lower_h(split, DC - 2)
                    early_lower_h(split, DC - 1)

            def add_chunks(stage):
                for c in range(DC):
                    b = full(stage, c)
                    dve.tensor_tensor(xT[:, c, :], xT[:, c, :], ps[:, b, 0:T], ALU.add).then_inc(dve_free, 1)
                dve.wait_ge(dve_free, D0[stage] + DC)
                dve.engine_nop().then_inc(x_ready, 1)

            dve.memset(stat[:], 1.0).then_inc(moved, 1)
            dve.engine_nop().then_inc(gate_free, CREDIT)
            dve.wait_ge(consts_loaded, 16 * 3)
            dve.tensor_copy(iota_top[:], iota[:, 0:TOP])
            dve.tensor_copy(iota16[:], iota[:])
            for k in range(NX):
                dve.wait_ge(x_loaded[k], 16)
            norm("na", 1, 0, split=0)
            dve.wait_ge(mix_loaded, 16 * 7)
            dve.tensor_tensor(wsp, wsp, maskp.unsqueeze(1).broadcast_to((P, AG, P)), ALU.mult)
            dve.tensor_tensor(wss[0:NSAMP], wss[0:NSAMP],
                              masks[0:NSAMP].unsqueeze(1).broadcast_to((NSAMP, AG, NSAMP)), ALU.mult).then_inc(ws_ready, 1)
            dve.wait_ge(v_square, 1)
            dve.tensor_scalar(stat[:, 3:6], stat[:, 0:3], 1.0 / DAV, EPS, ALU.mult, ALU.add).then_inc(ms_ready, 1)
            dve.wait_ge(root_ready, 2)
            link(dve.reciprocal(stat[:, 9:12], stat[:, 6:9]))
            newton(stat[:, 9:12], stat[:, 3:6], stat[:, 12:15])
            for m, (t0, tn) in enumerate(TILES):
                last = dve.scalar_tensor_tensor(out=v[0:tn, m, :], in0=v[0:tn, m, :], scalar=stat[0:tn, 9 + m:10 + m],
                                                in1=vgain[0:tn], op0=ALU.mult, op1=ALU.mult)
            last.then_inc(v_ready, 1)
            dve.wait_ge(act_free, A0["q0"])
            for c in range(FC):
                b = full("gate", c)
                g = c * P // 256
                dve.tensor_tensor(ps[:, b, 0:NPROMPT].rearrange("p (m t) -> p m t", m=2),
                                  ps[:, b, 0:NPROMPT].rearrange("p (m t) -> p m t", m=2),
                                  bsp[:, g:g + 1, :].broadcast_to((P, 2, P)), ALU.add)
                link(dve.tensor_tensor(ps[:, b, NPROMPT:T], ps[:, b, NPROMPT:T], bss[:, g, :], ALU.add))
                dve.tensor_tensor(uT[:, c, :], uT[:, c, :], ps[:, b, 0:T], ALU.mult).then_inc(dve_free, 1)
                dve.wait_ge(dve_free, D0["gate"] + c + 1)
                dve.engine_nop().then_inc(ug_ready, 1)
            add_chunks("wo")

            def peer(layer):
                norm(f"n{layer}", 3 + 2 * layer, 1 if layer == 0 else 4, split=(layer + 1) * DC)

                def take_wait():
                    dve.memset(stat[:, 15:16], 0.0)

                def top16(val, idx, src, n):
                    take_wait()
                    for a in range(n):
                        last = dve.max(val[:, a, 0:8], src[:, a, :])
                    link(last)
                    take_wait()
                    for a in range(n):
                        dve.max_index(idx[:, a, 0:8], val[:, a, 0:8], src[:, a, :])
                    for a in range(n):
                        last = dve.match_replace(src[:, a, :], val[:, a, 0:8], src[:, a, :], BIG)
                    link(last)
                    take_wait()
                    for a in range(n):
                        last = dve.max(val[:, a, 8:16], src[:, a, :])
                    link(last)
                    take_wait()
                    for a in range(n):
                        last = dve.max_index(idx[:, a, 8:16], val[:, a, 8:16], src[:, a, :])
                    return last

                def route(m, src, heads):
                    n = heads * TOP
                    link(top16(tv, ti, src, 2 * heads))
                    tv4 = tv.rearrange("p (h s) k -> p h s k", s=2)[:, 0:heads]
                    link(dve.tensor_tensor(cand[:, 0:heads].rearrange("p h (a b) -> p h a b", a=TOP),
                                           tv4[:, :, 0, :].unsqueeze(3).broadcast_to((P, heads, TOP, TOP)),
                                           tv4[:, :, 1, :].unsqueeze(2).broadcast_to((P, heads, TOP, TOP)), ALU.add))
                    link(top16(cs, pos.rearrange("p (a b) -> p a b", a=PH), cand, heads))
                    dve.tensor_tensor(gs[:, bass.ds(m * PH, heads), :], cs[:, 0:heads, :],
                                      cs[:, 0:heads, 0:1].broadcast_to((P, heads, TOP)), ALU.subtract)
                    dve.tensor_copy(tif.rearrange("p h s k -> p (h s k)")[:, 0:2 * n],
                                    ti.rearrange("p a b -> p (a b)")[:, 0:2 * n])
                    dve.tensor_scalar(pos12[:, 0, 0:n], pos[:, 0:n], 4, None, ALU.logical_shift_right)
                    link(dve.tensor_scalar(pos12[:, 1, 0:n], pos[:, 0:n], 15, None, ALU.bitwise_and))
                    link(dve.tensor_copy(posf[:, :, 0:n], pos12[:, :, 0:n]))
                    for s in range(2):
                        link(dve.tensor_tensor(eq[:, 0:n, :], posf[:, s, 0:n].unsqueeze(2).broadcast_to((P, n, TOP)),
                                               iota_top[:].unsqueeze(1).broadcast_to((P, n, TOP)), ALU.is_equal))
                        eq4 = eq.rearrange("p (h k) j -> p h k j", h=PH)[:, 0:heads]
                        link(dve.tensor_tensor(eq4, eq4,
                                               tif[:, 0:heads, s, :].unsqueeze(2).broadcast_to((P, heads, TOP, TOP)),
                                               ALU.mult))
                        link(dve.tensor_reduce(eg[:, bass.ds(m, 1), s, 0:n], eq[:, 0:n, :], AXX, ALU.add))

                def route_prompt(m):
                    link(dve.tensor_copy(S.rearrange("p a b -> p (a b)").unsqueeze(1), S2[:, bass.ds(m, 1), :]))
                    route(m, S, PH)

                dve.wait_ge(act_free, A0[f"U{layer}"])
                route(2, Ssam, SH)
                loop(2, 1 + 3 + 1 + 1 + 3 + 1 + 2 + 6, route_prompt)
                dve.wait_ge(dstep, count["n"])
                dve.engine_nop().then_inc(exp_in, 1)
                dve.wait_ge(exp_out, layer + 1)
                link(dve.tensor_reduce(gsum, gs, AXX, ALU.add))
                link(dve.reciprocal(grec, gsum))
                for m in range(3):
                    h = PH if m < 2 else SH
                    last = dve.tensor_tensor(eg[:, m, 2, 0:h * TOP].rearrange("p (h k) -> p h k", h=h),
                                             gs[:, m * PH:m * PH + h, :],
                                             grec[:, m * PH:m * PH + h].unsqueeze(2).broadcast_to((P, h, TOP)), ALU.mult)
                last.then_inc(slot_ready, 1)
                dve.memset(slots[:, :, T:3 * P], 0.0)
                for m, (t0, tn) in enumerate(TILES):
                    b = full(f"e{layer}", m)
                    dve.tensor_copy(slots[:, :, t0:t0 + tn],
                                    ps[:, b, 0:3 * tn].rearrange("p (a b) -> p a b", a=3)).then_inc(dve_free, 1)
                dve.wait_ge(dve_free, D0[f"e{layer}"] + 3)
                dve.tensor_copy(halves[:], slots[:, 0:2, :])
                for c in range(3):
                    link(dve.tensor_copy(parts[:, c, :], slots[:, 2, :]))
                    if c < 2:
                        link(dve.tensor_tensor(slots[:, 2, :], slots[:, 2, :], parts[:, c, :], ALU.subtract))

                def one_hot_group(q, j, it):
                    s = j % RH
                    tok = j * GT if it is None else it * (GR * GT) + j * GT
                    before = (layer * NQ + q) * (NGG + LEAD) + j
                    if before:
                        dve.wait_ge(hot_ready, before if it is None else it * GR + before)
                    step(dve.tensor_tensor(here2, iota16[:, q * EQ:(q + 1) * EQ].unsqueeze(1).broadcast_to((P, GT, EQ)),
                                           halves[:, 1, bass.ds(tok, GT)].unsqueeze(2).broadcast_to((P, GT, EQ)),
                                           ALU.is_equal))
                    dve.tensor_tensor(hot1[:, s], iota16[:].unsqueeze(1).broadcast_to((P, GT, NK)),
                                      halves[:, 0, bass.ds(tok, GT)].unsqueeze(2).broadcast_to((P, GT, NK)),
                                      ALU.is_equal)
                    last_step()
                    dve.tensor_tensor(hot2[:, s], here2.unsqueeze(1).broadcast_to((P, 3, GT, EQ)),
                                      parts[:, :, bass.ds(tok, GT)].unsqueeze(3).broadcast_to((P, 3, GT, EQ)),
                                      ALU.mult).then_inc(hot_ready, 1)

                def gate_groups(q, done, of, it):
                    if q is None:
                        return
                    nth = layer * NQ + q
                    for j in range(due(done, of, q), due(done + 1, of, q)):
                        dve.wait_ge(gate_full, it * GR + (nth * NGG + j + 1))
                        dst = C[:, q % 2, :, bass.ds(it * (GR * GT) + j * GT, GT)]
                        src = ps[:, 6 + j % 2, 0:GT * EQ].rearrange("p (t e) -> p e t", t=GT)
                        dve.tensor_tensor(dst, dst, src, ALU.mult).then_inc(gate_free, 1)
                        one_hot_group(q, j + LEAD, it)

                def quarter(q, gates):
                    k0 = None if q is None else D0[f"V{layer}"] + q * DC

                    def body(it):
                        for dc in range(4):
                            gate_groups(gates, dc, 4, it)
                            if q is not None:
                                dve.wait_ge(dve_full, it * 4 + (k0 + dc + 1))
                                dst = xT[:, bass.ds(it * 4 + dc, 1), :]
                                dve.tensor_tensor(dst, dst, ps[:, 4 + dc % 2:5 + dc % 2, 0:T],
                                                  ALU.add).then_inc(dve_free, 1)

                    if gates is not None:
                        for j in range(LEAD):
                            one_hot_group(gates, j, None)
                        dve.wait_ge(act_free, A0[f"U{layer}"] + (gates + 1) * EQ)
                    loop(2, GR if gates is not None else 0, body)

                def lower_C(q):
                    dve.wait_ge(gate_free, (layer * NQ + q + 1) * NGG + CREDIT)
                    for k, (e0, e1) in enumerate(CCHUNKS):
                        dve.wait_ge(C_hi_made, (layer * NQ + q) * len(CCHUNKS) + k + 1)
                        dve.tensor_tensor(C_lo[:, q % 2, e0:e1, :], C[:, q % 2, e0:e1, :], C_hi[:, e0:e1, :],
                                          ALU.subtract).then_inc(C_lo_made, 1)

                quarter(None, 0)
                for q in range(NQ):
                    lower_C(q)
                    quarter(q, q + 1 if q + 1 < NQ else None)
                dve.wait_ge(dve_free, D0[f"V{layer}"] + NQ * DC)
                dve.engine_nop().then_inc(x_ready, 1)

            peer(0)

            norm("nb", 4, 3)
            dve.wait_ge(act_free, A0["qn"])
            scaled(2)
            dve.wait_ge(act_free, A0["k"])
            dve.tensor_tensor(q_lo[:], qn, q_hi[:], ALU.subtract).then_inc(q_parts, 1)
            for b_ in range(NB):
                dve.wait_ge(k_landed[b_ % 2], 16 * NG * (b_ // 2 + 1))
                for g in range(NG):
                    n = CK[g]
                    for pr in range(2):
                        b = full("qk", (b_ * NG + g) * 2 + pr)
                        if CS[g] == 1:
                            keys = Kc[0:n, b_ % 2, 0:256].unsqueeze(1).broadcast_to((n, 2, 256))
                        else:
                            at = COFF[g] + 2 * pr * 256
                            keys = Kc[0:n, b_ % 2, at:at + 512].rearrange("p (a b) -> p a b", a=2)
                        dve.tensor_tensor(prod[0:n, 8 * pr:8 * pr + 8, :].rearrange("p (a h) e -> p a (h e)", a=2),
                                          keys, ps[0:n, b, :].rearrange("p (a b) -> p a b", a=2),
                                          ALU.mult).then_inc(dve_free, 1)
                    dve.wait_ge(dve_free, D0["qk"] + (b_ * NG + g) * 2 + 2)
                    out = Sk[0:n, g, :].rearrange("p (h t) -> p t h", h=HPG)[:, NS * b_:NS * b_ + NS, :]
                    last = dve.tensor_reduce(out, prod[0:n].rearrange("p (t h) e -> p t h e", h=HPG), AXX, ALU.add)
                    if g < NG - 1:
                        link(last)
                last.then_inc(k_used, 1)
                dve.wait_ge(k_used, b_ + 1)
            dve.wait_ge(sbias_loaded, 16)
            b = full("sc", 0)
            dve.tensor_tensor(Ss[:, 0:320], sbias[:, 0:320], ps[:, b, 0:320], ALU.add).then_inc(dve_free, 1)
            for par in range(2):
                b = full("sc", 1 + par)
                for h in (par, par + 2):
                    rows = slice(32 * h, 32 * h + 32)
                    last = dve.tensor_tensor(Ss[rows, 320:SCOLS], sbias[rows, 320:SCOLS], ps[rows, b, 0:96], ALU.add)
                last.then_inc(dve_free, 1)
            dve.wait_ge(dve_free, D0["ps"])
            link(dve.reduce_max(stat[:, 9:10], Ss, AXX))
            dve.tensor_scalar(stat[:, 9:10], stat[:, 9:10], -1.0, None, ALU.mult).then_inc(sm_in, 1)
            dve.wait_ge(sm_exp, 1)
            link(dve.reciprocal(stat[:, 10:11], stat[:, 10:11]))
            dve.tensor_scalar(Ss, Ss, stat[:, 10:11], None, ALU.mult).then_inc(sm_out, 1)
            dve.wait_ge(dist_loaded, 16)

            def unit_scores(u):
                h, m = u // 2, u % 2
                n = P * (m + 1)
                if u >= 2:
                    dve.wait_ge(act_free, A0["pp"] + sum(3 if w % 2 else 2 for w in range(u - 1)))
                for g in range(NG):
                    b = full("ps", 3 * u + g)
                    dve.scalar_tensor_tensor(out=Pps[m][:, g, 0:n], in0=dist[:, g, m, 0:n], scalar=SLOPES[g * HPG + h],
                                             in1=ps[:, b, 0:n], op0=ALU.mult, op1=ALU.add).then_inc(dve_free, 1)
                dve.wait_ge(dve_free, D0["ps"] + 3 * u + 3)
                top = stat[:, 11 + 2 * m:12 + 2 * m]
                link(dve.tensor_reduce(top, Pps[m][:, :, 0:n], mybir.AxisListType.XY, ALU.max))
                dve.tensor_scalar(top, top, -1.0, None, ALU.mult).then_inc(pp_in, 1)

            unit_scores(0)
            for u in range(8):
                m = u % 2
                n = P * (m + 1)
                if u + 1 < 8:
                    unit_scores(u + 1)
                total = stat[:, 12 + 2 * m:13 + 2 * m]
                dve.wait_ge(pp_exp, u + 1)
                link(dve.reciprocal(total, total))
                dve.tensor_scalar(Pps[m][:, :, 0:n], Pps[m][:, :, 0:n], total, None, ALU.mult).then_inc(pp_out, 1)
            add_chunks("ob")
            peer(1)
            norm("nf", 6, 5)


def _lhs_blocks(w):
    m = w.shape[1] // 256
    return w.reshape(8, 128, m, 2, 128).transpose(2, 1, 3, 0, 4).reshape(m, 128, 2048)


def _constants():
    r = np.arange(128)
    out = {"ident": np.eye(128), "iota": np.tile(r, (128, 1)), "maskp": r[:, None] <= r[None, :]}
    s = np.arange(32)
    out["masks"] = (s[:, None] // 4 == s[None, :] // 4) & (s[:, None] <= s[None, :])
    dist = np.zeros((128, 3, 2, 256))
    for g, (w, d) in enumerate(zip(WINDOWS, DILS)):
        i, j = np.arange(256)[:, None], np.arange(256)[None, :]
        ok = (j <= i) & ((i - j) % d == 0) & (i - j <= w)
        dist[:, g] = np.where(ok, -(i - j), -1e30).reshape(2, 128, 256).transpose(1, 0, 2)
    out["dist"] = dist
    bias = np.zeros((4, 32, SCOLS))
    for h in range(4):
        for t in range(32):
            b, s_ = divmod(t, 4)
            row = bias[h, t]
            k = np.arange(128)
            row[0:128] = np.where(k >= s_, -SLOPES[h] * (128 + s_ - k), -1e30)
            row[128:256] = -SLOPES[4 + h] * 4 * (128 - k)
            k = np.arange(64)
            row[256:320] = -SLOPES[8 + h] * 16 * (64 - k)
            n = np.arange(32)
            row[320:352] = np.where((n // 4 == b) & (n <= t), -SLOPES[h] * (t - n), -1e30)
            row[352:384] = np.where(n == t, 0.0, -1e30)
            row[384:416] = np.where(n == t, 0.0, -1e30)
    out["sbias"] = bias.reshape(128, SCOLS)
    return {k: np.ascontiguousarray(v, dtype=np.float32) for k, v in out.items()}


def _layout(a):
    x = np.concatenate([a["x_prompt"].reshape(256, 1024), a["x_sample"].reshape(32, 1024)])
    i = dict(_constants())
    i["xT"] = x.T.reshape(8, 128, 288).transpose(1, 0, 2)
    g = np.stack([a["a_norm"][0], a["ffn_norm"][0], a["kv_norm"], a["b_norm"][0], a["ffn_norm"][1], a["final_norm"]])
    i["gains"] = g.reshape(6, 8, 128).transpose(2, 0, 1)
    i["vgain"] = a["a_v_norm"][0]
    w_in = a["a_w_in"][0]
    i["w_in_u"] = _lhs_blocks(w_in[:, :2048])
    i["w_in_v"] = w_in[:, 2048:].reshape(2, 4, 128, 4, 512).transpose(3, 0, 2, 1, 4).reshape(8, 128, 2048)
    ws = a["a_w_s"][0]
    i["wsp"] = ws.transpose(2, 0, 1)
    i["wss"] = np.tile(ws[:, :4, :4].transpose(2, 0, 1), (8, 1, 8))
    i["bsp"] = a["a_b_s"][0]
    i["bss"] = np.tile(a["a_b_s"][0][:, :4], (1, 8))
    i["w_out"] = a["a_w_out"][0].reshape(16, 128, 8, 128).transpose(2, 1, 0, 3).reshape(8, 128, 2048)
    i["w_k"] = _lhs_blocks(a["w_kv"][:, :768])
    i["w_v"] = a["w_kv"][:, 768:].reshape(8, 128, 3, 256).transpose(2, 1, 0, 3).reshape(3, 128, 2048)
    i["w_q"] = _lhs_blocks(a["b_w_q"][0])
    i["w_o"] = a["b_w_o"][0].reshape(6, 128, 8, 128).transpose(1, 2, 0, 3).reshape(128, 3, 2048).transpose(1, 0, 2)
    i["skT"] = a["peer_sub_keys"].transpose(3, 0, 1, 2)
    for n in range(2):
        i[f"peer_q{n}"] = _lhs_blocks(a["peer_w_q"][n])
        i[f"U{n}"] = a["peer_u"][n].reshape(128, 64, 2, 8, 128).transpose(1, 4, 2, 3, 0).reshape(64, 128, 2048)
        i[f"V{n}"] = a["peer_v"][n].reshape(128, 4, 2, 16, 8, 128).transpose(1, 4, 2, 0, 3, 5).reshape(64, 128, 2048)
    for n, w in enumerate((128, 512, 2048)):
        c = a[f"cache_kv_w{w}"]
        i[f"cache{n}"] = c.reshape(8, c.shape[1], 2, 256)
    return i


_OUTS = {"yT": (128, 8, 288), "a_v_prompt": (128, 2048), "a_v_sample": (32, 2048), "kT": (128, 6, 288),
         "v_prompt": (128, 2, 768), "v_sample": (32, 768)}


def kernel(**inputs):
    import concourse.bacc as _bacc
    from concourse.bass_utils import run_bass_kernel_spmd as _run

    laid = {k: np.ascontiguousarray(v) for k, v in _layout({k: np.asarray(v) for k, v in inputs.items()}).items()}
    nc = _bacc.Bacc("TRN2", target_bir_lowering=False, num_devices=1)
    ins = {k: nc.dram_tensor(f"in_{k}", v.shape, mybir.dt.from_np(v.dtype), kind="ExternalInput").ap()
           for k, v in laid.items()}
    outs = {k: nc.dram_tensor(f"out_{k}", s, F32, kind="ExternalOutput").ap() for k, s in _OUTS.items()}
    build(nc, ins, outs)
    r = _run(nc, [{f"in_{k}": v for k, v in laid.items()}], core_ids=[0]).results[0]
    y = r["out_yT"].transpose(2, 1, 0).reshape(288, 1024)
    k = r["out_kT"].transpose(2, 1, 0).reshape(288, 3, 4, 64)
    v = np.concatenate([r["out_v_prompt"].transpose(1, 0, 2).reshape(256, 768), r["out_v_sample"]]).reshape(288, 3, 4, 64)
    kv = np.stack([k, v], axis=1)
    prompt, sample = kv[None, :256], kv[256:].reshape(8, 4, 2, 3, 4, 64)
    return (y[None, :256], y[256:].reshape(8, 4, 1024),
            r["out_a_v_prompt"][None, None], r["out_a_v_sample"].reshape(1, 8, 4, 2048),
            prompt[:, 128:, :, 0], prompt[:, :, :, 1], prompt[:, :, :, 2],
            sample[:, :, :, 0], sample[:, :, :, 1], sample[:, :, :, 2])
```
